# Optimizing a Trainium2 kernel written in Bass

```python
import math
import jax
import jax.numpy as jnp
from jax import lax
import numpy as np

D_MODEL = 1024
BATCH = 1
SEQ = 512
DEPTH = 1
DEC_BATCH = 8
DEC_SEQ = 8
PAST_LEN = 4096
PAGE_SIZE = 128

D_MIX = D_MODEL
D_HGRN = D_MIX // 2
HGRN_HEADS = 4
HGRN_DK = D_HGRN // HGRN_HEADS
HGRN_DV = D_HGRN // HGRN_HEADS
HGRN_CHUNK = 32
D_SSM = D_MIX - D_HGRN
SSM_GROUP = 16
SSM_GROUPS = D_SSM // SSM_GROUP
SSM_STATE = 64
D_IN = 4 * D_HGRN + D_SSM
MOE_GROUPS = 4
MOE_PER_GROUP = 8
MOE_TOP_K = 2
D_EXPERT = D_MODEL // 4
EPS = 1e-6
DT_MIN = 1e-3
DT_MAX = 1e-1
MAX_REAL = -1e-4

kernel_name = 'hybrid_hgrn2_s5_hmoe_step'

def _rms(x):
    x = x.astype(jnp.float32)
    return x * lax.rsqrt(jnp.mean(x * x, axis=-1, keepdims=True) + EPS)

def _adanorm(x, gain, shift, scale):
    h = _rms(x) * gain.astype(jnp.float32)
    return (h * (1.0 + scale[:, None, :]) + shift[:, None, :]).astype(x.dtype)

def _hgrn2_recurrence(q, k, v, logf, s0):
    bsz, t, nh, _ = q.shape
    dv = v.shape[-1]
    c = HGRN_CHUNK
    n = -(-t // c)
    pad = n * c - t

    def blocks(a):
        a = jnp.pad(a, ((0, 0), (0, pad), (0, 0), (0, 0)))
        return a.reshape(bsz, n, c, nh, a.shape[-1]).transpose(1, 0, 3, 2, 4)

    causal = jnp.tril(jnp.ones((c, c), dtype=bool))[:, :, None]

    def step(state, blk):
        qb, kb, vb, gb = blk
        cum = jnp.cumsum(gb, axis=2)
        rel = cum[:, :, :, None, :] - cum[:, :, None, :, :]
        decay = jnp.exp(jnp.where(causal, rel, -jnp.inf))
        scores = jnp.einsum('bhtk,bhsk,bhtsk->bhts', qb, kb, decay)
        o = (jnp.einsum('bhts,bhsv->bhtv', scores, vb)
             + jnp.einsum('bhtk,bhkv->bhtv', qb * jnp.exp(cum), state))
        last = cum[:, :, -1:, :]
        state = (jnp.exp(last[:, :, 0, :, None]) * state
                 + jnp.einsum('bhsk,bhsv->bhkv', kb * jnp.exp(last - cum), vb))
        return state, o

    s_final, o = lax.scan(step, s0, (blocks(q), blocks(k), blocks(v), blocks(logf)))
    o = o.transpose(1, 0, 3, 2, 4).reshape(bsz, n * c, nh, dv)[:, :t]
    return o, s_final

def _complex_affine_combine(e1, e2):
    a1r, a1i, b1r, b1i = e1
    a2r, a2i, b2r, b2i = e2
    return (a2r * a1r - a2i * a1i,
            a2r * a1i + a2i * a1r,
            a2r * b1r - a2i * b1i + b2r,
            a2r * b1i + a2i * b1r + b2i)

def _s5_mixer(u, s_re, s_im, p):
    f32 = jnp.float32
    bsz, t, _ = u.shape
    ug = u.astype(f32).reshape(bsz, t, SSM_GROUPS, SSM_GROUP)
    lam_re = jnp.minimum(p['ssm_a_re'].astype(f32), MAX_REAL)
    lam_im = p['ssm_a_im'].astype(f32)
    dt = jnp.exp(p['ssm_log_dt'].astype(f32))
    mag = jnp.exp(lam_re * dt)
    abar_re = mag * jnp.cos(lam_im * dt)
    abar_im = mag * jnp.sin(lam_im * dt)
    den = lam_re * lam_re + lam_im * lam_im
    coef_re = ((abar_re - 1.0) * lam_re + abar_im * lam_im) / den
    coef_im = (abar_im * lam_re - (abar_re - 1.0) * lam_im) / den
    b_re = p['ssm_b_re'].astype(f32)
    b_im = p['ssm_b_im'].astype(f32)
    bbar_re = coef_re[..., None] * b_re - coef_im[..., None] * b_im
    bbar_im = coef_re[..., None] * b_im + coef_im[..., None] * b_re
    bu_re = jnp.einsum('btgh,gph->btgp', ug, bbar_re)
    bu_im = jnp.einsum('btgh,gph->btgp', ug, bbar_im)
    x0_re = s_re.astype(f32)
    x0_im = s_im.astype(f32)
    bu_re = bu_re.at[:, 0].add(abar_re * x0_re - abar_im * x0_im)
    bu_im = bu_im.at[:, 0].add(abar_re * x0_im + abar_im * x0_re)
    a_re = jnp.broadcast_to(abar_re, bu_re.shape)
    a_im = jnp.broadcast_to(abar_im, bu_im.shape)
    _, _, xs_re, xs_im = lax.associative_scan(_complex_affine_combine, (a_re, a_im, bu_re, bu_im), axis=1)
    y = (jnp.einsum('btgp,ghp->btgh', xs_re, p['ssm_c_re'].astype(f32))
         - jnp.einsum('btgp,ghp->btgh', xs_im, p['ssm_c_im'].astype(f32))
         + p['ssm_d'].astype(f32) * ug)
    y = jax.nn.gelu(y).reshape(bsz, t, D_SSM)
    y = y * jax.nn.sigmoid(jnp.dot(y, p['ssm_w_glu'].astype(f32)) + p['ssm_b_glu'].astype(f32))
    y = _rms(y) * p['ssm_norm'].astype(f32)
    return y, xs_re[:, -1], xs_im[:, -1]

def _hier_moe(h, p):
    f32 = jnp.float32
    bsz, t, d = h.shape
    xt = h.reshape(bsz * t, d)
    grp_logits = (jnp.dot(xt, p['moe_w_group']) + p['moe_b_group']).astype(f32)
    grp_prob = jax.nn.softmax(grp_logits, axis=-1)
    grp_onehot = jax.nn.one_hot(jnp.argmax(grp_logits, axis=-1), MOE_GROUPS, dtype=f32)
    grp_w = jnp.sum(grp_prob * grp_onehot, axis=-1)
    exp_logits = (jnp.einsum('nd,gde->nge', xt, p['moe_w_router']) + p['moe_b_router']).astype(f32)
    sel_logits = jnp.einsum('nge,ng->ne', exp_logits, grp_onehot)
    top_val, top_idx = lax.top_k(sel_logits, MOE_TOP_K)
    top_w = jax.nn.softmax(top_val, axis=-1) * grp_w[:, None]
    within = jnp.einsum('nk,nke->ne', top_w, jax.nn.one_hot(top_idx, MOE_PER_GROUP, dtype=f32))
    combine = grp_onehot[:, :, None] * within[:, None, :]
    out = jnp.zeros((bsz * t, d), f32)
    for g in range(MOE_GROUPS):
        a = jnp.einsum('nd,edf->nef', xt, p['moe_w_gate'][g])
        b = jnp.einsum('nd,edf->nef', xt, p['moe_w_up'][g])
        act = jax.nn.silu(a) * b * combine[:, g, :, None].astype(a.dtype)
        out = out + jnp.einsum('nef,efd->nd', act, p['moe_w_down'][g])
    return out.reshape(bsz, t, d)

def _layer(x, c, s_h, s_re, s_im, lb, p):
    f32 = jnp.float32
    bsz, t, _ = x.shape
    ada = (jnp.dot(jax.nn.silu(c), p['w_ada']) + p['b_ada']).astype(f32)
    shift1, scale1, gate1, shift2, scale2, gate2 = jnp.split(ada, 6, axis=-1)
    h = _adanorm(x, p['norm_mix'], shift1, scale1)
    proj = jnp.einsum('btd,de->bte', h, p['w_in'])
    q_raw, f_raw, i_raw, g_raw, u = jnp.split(proj, [D_HGRN, 2 * D_HGRN, 3 * D_HGRN, 4 * D_HGRN], axis=-1)

    def heads(a):
        return a.astype(f32).reshape(bsz, t, HGRN_HEADS, -1)
    f = lb + (1.0 - lb) * jax.nn.sigmoid(f_raw.astype(f32))
    q = heads(jax.nn.silu(q_raw.astype(f32))) * (HGRN_DK ** -0.5)
    o_h, s_h_new = _hgrn2_recurrence(q, heads(1.0 - f), heads(i_raw), heads(jnp.log(f)), s_h.astype(f32))
    o_h = (_rms(o_h) * p['hgrn_norm'].astype(f32).reshape(HGRN_HEADS, HGRN_DV)).reshape(bsz, t, D_HGRN)
    o_h = o_h * jax.nn.silu(g_raw.astype(f32))

    o_s, s_re_new, s_im_new = _s5_mixer(u, s_re, s_im, p)

    mix = jnp.concatenate([o_h, o_s], axis=-1).astype(x.dtype)
    x = x + (gate1[:, None, :] * jnp.einsum('bte,ed->btd', mix, p['w_out'])).astype(x.dtype)
    h = _adanorm(x, p['norm_ffn'], shift2, scale2)
    x = x + (gate2[:, None, :] * _hier_moe(h, p)).astype(x.dtype)
    return x, s_h_new, s_re_new, s_im_new

def _trunk(x, c, s_h, s_re, s_im, lower_bounds, layer_params, w_ada_final, b_ada_final, norm_final):
    hs, res, ims = [], [], []
    for l in range(DEPTH):
        x, a, b, d = _layer(x, c, s_h[l], s_re[l], s_im[l], lower_bounds[l], layer_params[l])
        hs.append(a.astype(x.dtype))
        res.append(b.astype(x.dtype))
        ims.append(d.astype(x.dtype))
    ada = (jnp.dot(jax.nn.silu(c), w_ada_final) + b_ada_final).astype(jnp.float32)
    shift, scale = jnp.split(ada, 2, axis=-1)
    y = _adanorm(x, norm_final, shift, scale)
    return y, jnp.stack(hs), jnp.stack(res), jnp.stack(ims)

def setup_inputs(seed: int = 0) -> dict:
    key = jax.random.key(seed)
    ks = iter(jax.random.split(key, 64))
    f32 = jnp.float32
    d, L = D_MODEL, DEPTH
    G, P, H = SSM_GROUPS, SSM_STATE, SSM_GROUP

    def normal(shape, scale):
        return jax.random.normal(next(ks), shape, f32) * scale

    def gain(shape):
        return 1.0 + normal(shape, 0.01)

    out = {}
    out['x_prompt'] = normal((BATCH, SEQ, d), 1.0)
    out['x_sample'] = normal((DEC_BATCH, DEC_SEQ, d), 1.0)
    out['c_prompt'] = normal((BATCH, d), 1.0)
    out['c_sample'] = normal((DEC_BATCH, d), 1.0)
    out['state_hgrn'] = normal((L, DEC_BATCH, HGRN_HEADS, HGRN_DK, HGRN_DV), 0.5)
    out['state_ssm_re'] = normal((L, DEC_BATCH, G, P), 0.1)
    out['state_ssm_im'] = normal((L, DEC_BATCH, G, P), 0.1)
    out['hgrn_lb_logits'] = normal((L + 1, D_HGRN), 0.1)
    out['w_ada'] = normal((L, d, 6 * d), 0.2 * d ** -0.5)
    out['b_ada'] = normal((L, 6 * d), 0.02)
    out['norm_mix'] = gain((L, d))
    out['w_in'] = normal((L, d, D_IN), d ** -0.5)
    out['hgrn_norm'] = gain((L, D_HGRN))
    out['ssm_a_re'] = -0.5 + normal((L, G, P), 0.01)
    out['ssm_a_im'] = math.pi * jnp.arange(P, dtype=f32) + normal((L, G, P), 0.01)
    out['ssm_log_dt'] = jax.random.uniform(next(ks), (L, G, P), f32, math.log(DT_MIN), math.log(DT_MAX))
    out['ssm_b_re'] = normal((L, G, P, H), (2.0 * H) ** -0.5)
    out['ssm_b_im'] = normal((L, G, P, H), (2.0 * H) ** -0.5)
    out['ssm_c_re'] = normal((L, G, H, P), (2.0 * P) ** -0.5)
    out['ssm_c_im'] = normal((L, G, H, P), (2.0 * P) ** -0.5)
    out['ssm_d'] = normal((L, G, H), 1.0)
    out['ssm_w_glu'] = normal((L, D_SSM, D_SSM), D_SSM ** -0.5)
    out['ssm_b_glu'] = normal((L, D_SSM), 0.01)
    out['ssm_norm'] = gain((L, D_SSM))
    out['w_out'] = normal((L, D_MIX, d), D_MIX ** -0.5)
    out['norm_ffn'] = gain((L, d))
    out['moe_w_group'] = normal((L, d, MOE_GROUPS), d ** -0.5)
    out['moe_b_group'] = normal((L, MOE_GROUPS), 0.01)
    out['moe_w_router'] = normal((L, MOE_GROUPS, d, MOE_PER_GROUP), d ** -0.5)
    out['moe_b_router'] = normal((L, MOE_GROUPS, MOE_PER_GROUP), 0.01)
    out['moe_w_gate'] = normal((L, MOE_GROUPS, MOE_PER_GROUP, d, D_EXPERT), d ** -0.5)
    out['moe_w_up'] = normal((L, MOE_GROUPS, MOE_PER_GROUP, d, D_EXPERT), d ** -0.5)
    out['moe_w_down'] = normal((L, MOE_GROUPS, MOE_PER_GROUP, D_EXPERT, d), D_EXPERT ** -0.5)
    out['w_ada_final'] = normal((d, 2 * d), 0.2 * d ** -0.5)
    out['b_ada_final'] = normal((2 * d,), 0.02)
    out['norm_final'] = gain((d,))
    return out

def reference(x_prompt, x_sample, c_prompt, c_sample, state_hgrn, state_ssm_re, state_ssm_im,
              hgrn_lb_logits, w_ada, b_ada, norm_mix, w_in, hgrn_norm,
              ssm_a_re, ssm_a_im, ssm_log_dt, ssm_b_re, ssm_b_im, ssm_c_re, ssm_c_im, ssm_d,
              ssm_w_glu, ssm_b_glu, ssm_norm, w_out, norm_ffn,
              moe_w_group, moe_b_group, moe_w_router, moe_b_router, moe_w_gate, moe_w_up, moe_w_down,
              w_ada_final, b_ada_final, norm_final):
    lower_bounds = jnp.cumsum(jax.nn.softmax(hgrn_lb_logits.astype(jnp.float32), axis=0), axis=0)
    layer_params = [dict(w_ada=w_ada[l], b_ada=b_ada[l], norm_mix=norm_mix[l], w_in=w_in[l],
                         hgrn_norm=hgrn_norm[l], ssm_a_re=ssm_a_re[l], ssm_a_im=ssm_a_im[l],
                         ssm_log_dt=ssm_log_dt[l], ssm_b_re=ssm_b_re[l], ssm_b_im=ssm_b_im[l],
                         ssm_c_re=ssm_c_re[l], ssm_c_im=ssm_c_im[l], ssm_d=ssm_d[l],
                         ssm_w_glu=ssm_w_glu[l], ssm_b_glu=ssm_b_glu[l], ssm_norm=ssm_norm[l],
                         w_out=w_out[l], norm_ffn=norm_ffn[l],
                         moe_w_group=moe_w_group[l], moe_b_group=moe_b_group[l],
                         moe_w_router=moe_w_router[l], moe_b_router=moe_b_router[l],
                         moe_w_gate=moe_w_gate[l], moe_w_up=moe_w_up[l], moe_w_down=moe_w_down[l])
                    for l in range(DEPTH)]
    bp = x_prompt.shape[0]
    zeros_h = jnp.zeros((DEPTH, bp, HGRN_HEADS, HGRN_DK, HGRN_DV), jnp.float32)
    zeros_s = jnp.zeros((DEPTH, bp, SSM_GROUPS, SSM_STATE), jnp.float32)
    y_prompt, hgrn_prompt, ssm_re_prompt, ssm_im_prompt = _trunk(
        x_prompt, c_prompt, zeros_h, zeros_s, zeros_s, lower_bounds, layer_params,
        w_ada_final, b_ada_final, norm_final)
    y_sample, hgrn_sample, ssm_re_sample, ssm_im_sample = _trunk(
        x_sample, c_sample, state_hgrn, state_ssm_re, state_ssm_im, lower_bounds, layer_params,
        w_ada_final, b_ada_final, norm_final)
    return (y_prompt, y_sample, hgrn_prompt, ssm_re_prompt, ssm_im_prompt, hgrn_sample, ssm_re_sample, ssm_im_sample)


_drawn_inputs = setup_inputs


def setup_inputs(seed=0):
    import zlib

    import numpy as np

    out = dict(_drawn_inputs(seed))
    spreads = {}
    factors = {'norm_mix': 5.414,
     'hgrn_norm': 8.0,
     'ssm_a_re': 3.922,
     'ssm_c_re': 8.0,
     'ssm_c_im': 8.0,
     'ssm_b_glu': 8.0,
     'ssm_norm': 8.0,
     'norm_ffn': 8.0,
     'moe_b_group': 8.0,
     'moe_b_router': 8.0,
     'norm_final': 5.899}
    for name, (base, spread) in spreads.items():
        noise = np.random.default_rng([zlib.crc32(name.encode()), seed]).standard_normal(out[name].shape)
        drawn = base * np.exp(spread * noise) if base else spread * noise
        out[name] = jnp.asarray(drawn.astype(out[name].dtype))
    for name, factor in factors.items():
        out[name] = (out[name] * factor).astype(out[name].dtype)
    return out
```

```python
from contextlib import ExitStack

import concourse.bass as bass
from concourse import mybir

F32 = mybir.dt.float32
U32 = mybir.dt.uint32
I32 = mybir.dt.int32
ALU = mybir.AluOpType
ACT = mybir.ActivationFunctionType
AX = mybir.AxisListType.X
PI = 3.141592653589793


def decoder_step(nc, a, o):
    P = 128
    D = a["x_prompt"].shape[2]
    TP = a["x_prompt"].shape[1]
    NB, TS = a["x_sample"].shape[0], a["x_sample"].shape[1]
    NS = NB * TS
    NT = TP + NS
    PT = TP // P
    TILES = PT + 1
    ROWS = [P] * PT + [NS]
    C9 = 1 + NB
    KC = D // P
    H = a["state_hgrn"].shape[2]
    DH = H * P
    CH = 32
    NCH = TP // CH
    G, NP = a["ssm_a_re"].shape[1:]
    GH = a["ssm_d"].shape[2]
    NPAIR = G // 2
    SF = G * GH // P
    L = 8
    NC = NT // L
    PC = TP // L
    NG, NE = a["moe_w_gate"].shape[1:3]
    E = NG * NE
    DE = a["moe_w_gate"].shape[4]
    EPS = 1e-6

    with ExitStack() as ctx:
        def sem(name):
            return ctx.enter_context(nc.semaphore(name))

        SLOT = KC * 512
        SLOTS = 6
        total = 53200
        sb = ctx.enter_context(nc.sbuf_tensor("sb", [P, total], F32))
        top = [SLOTS * SLOT]

        def take(n):
            top[0] += n
            assert top[0] <= total, top[0]
            return top[0] - n

        def at(off, n, rows=P):
            return sb[0:rows, off:off + n]

        def v2(off, n1, n2, rows=P):
            return at(off, n1 * n2, rows).rearrange("p (a b) -> p a b", a=n1)

        def v3(off, n1, n2, n3, rows=P):
            return at(off, n1 * n2 * n3, rows).rearrange("p (a b c) -> p a b c", a=n1, b=n2)

        slot = [at(k * SLOT, SLOT) for k in range(SLOTS)]
        EXT = 4 * SLOT

        MIXT = take(KC * NT)
        mixT = v2(MIXT, KC, NT)
        MAIN = take(0)
        F_, Q_, U_ = take(H * NT), take(H * NT), take(H * NT)
        V_, G_ = take(TILES * DH), take(TILES * DH)
        HT = take(KC * NT)
        hT = v2(HT, KC, NT)
        fT, qT, uT = v2(F_, H, NT), v2(Q_, H, NT), v2(U_, SF, NT)
        V, Gt = v2(V_, TILES, DH), v2(G_, TILES, DH)
        ROWS8 = take(2 * D)
        rows8 = v2(ROWS8, 2, D)

        ident = at(take(P), P)
        ones = at(take(P), P)
        MASKP = take(P)
        maskP = at(MASKP, P)
        maskS = at(take(NS), NS, NS)
        seqm = at(take(NB), NB, NS)

        BIAS = take(512)
        bias16 = at(BIAS, 512, 16)
        adaT = v3(take(2 * KC * C9), 2, KC, C9)
        A1 = v2(take(KC * C9), KC, C9)
        gmixT = at(take(KC), KC)
        PARAMS = 80
        PROW = MIXT + 3904 + NT
        prow = at(PROW, P, PARAMS)
        prm = at(take(PARAMS), PARAMS)
        ghg = at(take(DH), DH)
        cT = v2(take(KC * C9), KC, C9)
        brt = at(take(NG + E), NG + E)
        ss = at(take(8), 8)
        rs = at(take(8), 8)
        lb = at(take(H), H)
        noml = at(take(H), H)
        oml = at(take(H), H)
        OV = top[0]
        Pw = [v2(take((L + 1) * NPAIR), L + 1, NPAIR) for _ in range(2)]
        BB = [v2(take(NPAIR * GH), NPAIR, GH) for _ in range(2)]
        CT = [v2(take(NPAIR * GH), NPAIR, GH) for _ in range(2)]
        X0 = [v2(take(NB * NPAIR), NB, NPAIR) for _ in range(2)]
        fin = [v2(take(C9 * NPAIR), C9, NPAIR) for _ in range(2)]
        PT_ = take(NPAIR * 24)
        par = [at(PT_ + NPAIR * k, NPAIR) for k in range(24)]
        PwR = [v2(take(L * NPAIR), L, NPAIR) for _ in range(2)]
        ov_end = top[0]
        dl = v2(take(H * NCH), H, NCH)
        dls = v2(take(H * NB), H, NB)
        comb = v2(take(TILES * E), TILES, E)
        before = maskP
        SM, rk = v2(take(TILES * E), TILES, E), v2(take(TILES * E), TILES, E)
        SMsum = v2(take((PT - 1) * E), PT - 1, E)
        pos = [at(take(TILES), TILES) for _ in range(2)]
        ypos = [at(take(TILES), TILES) for _ in range(2)]
        cntf, yoff, yix, xix = (at(take(E), E) for _ in range(4))
        pcol, tokid, flagf, flag = at(take(1), 1), at(take(TILES), TILES), at(take(1), 1), at(take(1), 1)
        top[0] = OV
        gfin = at(take(D), D)
        wgrp = v2(take(KC * NG), KC, NG)
        wrt = v3(take(NG * KC * NE), NG, KC, NE)
        wrc = v2(take(KC * (NG + E)), KC, NG + E)
        rt = take(600)
        o_rt = [rt]

        def rtile(n_):
            o_rt[0] += n_
            assert o_rt[0] <= rt + 600
            return o_rt[0] - n_

        RT = {}
        RT["gl"] = v2(rtile(TILES * 8), TILES, 8)
        RT["ge"] = v2(rtile(TILES * NG), TILES, NG)
        for nm in ("ngm", "gs", "gw", "dv", "e1", "w0", "w1", "gi", "i0", "i1"):
            RT[nm] = at(rtile(TILES), TILES)
        RT["el"] = v2(rtile(TILES * E), TILES, E)
        for nm in ("gm8", "sel", "sm8", "gx", "sx", "st"):
            RT[nm] = v2(rtile(TILES * 8), TILES, 8)
        RT["oh"] = v2(rtile(TILES * NG), TILES, NG)
        iota = at(take(E), E)
        iota_i = at(take(E), E)
        cb2 = v2(take(TILES * E), TILES, E)
        assert top[0] <= ov_end

        xin = v2(EXT, TILES, D)
        R_ = EXT + TILES * D
        R = [v2(R_ + k * NPAIR * PC, NPAIR, PC) for k in range(2)]
        junk = at(MIXT, D)
        C9IN = MIXT + D
        c9 = at(C9IN, D, C9)
        c9s = at(C9IN + D, D, C9)
        crow = v2(V_ + 2048, 4, P)
        bin_ = [v2(V_ + 2560 + 256 * k, NPAIR, GH) for k in range(2)]
        xrow = v2(V_ + 3072, 2, P)

        AB = [v3(V_ + 1024 * k, 4, L, 2 * GH) for k in range(2)]
        Bl = [v3(V_ + 2048 + 1024 * k, 4, 2, P) for k in range(2)]
        qraw = at(V_ + 4096, NT)
        cmask = at(EXT + 4480, NT)
        CA = [v3(EXT + 1152 * k, 4, L + 1, 2 * GH) for k in range(2)]
        Tm = v2(EXT + 2304, 4, 2 * P)
        Um = v3(EXT + 3328, 4, 2, NC)
        tq = [MIXT + 576 * k for k in range(4)]
        Z_ = [v2(MIXT + 2304 + 256 * k, 4, PC) for k in range(2)]
        Wp = [v2(MIXT + 2816 + 256 * k, 4, PC) for k in range(2)]
        Xb = [v2(MIXT + 3328 + 288 * k, 4, NC) for k in range(2)]

        Qt = v2(MIXT + 4 * NT, H, NT)
        sT = [v2(HT + 2304 + 512 * k, H, P) for k in range(2)]
        QhM = v3(HT + 3328, H, 4, NS)
        KhT = v2(EXT, TILES, DH)
        Sr = [v2(EXT + 2560 + 512 * k, H, P) for k in range(3)]
        mtok = [at(EXT + 4096 + 512 * k, DH) for k in range(2)]
        TMP = EXT + 5120
        cum, d1, d2, Ex, Kh = [at(TMP + NT * k, NT) for k in range(5)]
        S0 = [v3(off, 4, H, P) for off in (TMP, OV)]
        Vm = v2(HT, 4, DH)
        sq1 = at(TMP + 2880, P)

        y2 = v2(HT, SF, NT)
        sqy = v2(HT + 2304, SF, NT)
        rsy = at(G_ + D, NT)

        x = v2(MAIN, TILES, D)
        acc = v2(MAIN + TILES * D, TILES, D)
        g1b = v2(MAIN + TILES * D + 2 * D, 2, D)
        g2b = v2(MAIN + 2 * TILES * D, 2, D)
        sfb = v2(MAIN + 2 * TILES * D + 2 * D, 2, D)
        cfb = v2(MAIN + 2 * TILES * D + 4 * D, 2, D)
        xn2 = [at(MAIN + TILES * D + D * k, D) for k in range(2)]
        gffn = at(MAIN + TILES * D + 4 * D, D)
        B2b, A2b = sfb, cfb
        XG = MAIN + TILES * D
        xg = [at(XG + D * k, D) for k in range(2)]
        xT = [v2(XG + 2 * D + D * k, KC, P) for k in range(2)]
        yb = [at(MIXT + D * k, D) for k in range(2)]
        y1 = [at(D * t, D) for t in range(TILES)]
        h2T = mixT
        LG = NG + E
        lgT = at(MAIN + TILES * D + 2 * D, NT, LG)
        sg = [at(ROWS8 + 256 * k, DE) for k in range(2)]
        aa = [at(ROWS8 + 512 + 256 * k, DE) for k in range(2)]
        aT = [v2(ROWS8 + 1024 + 256 * k, 2, P) for k in range(2)]
        assert 2 * TILES * D + 6 * D <= HT + KC * NT - MAIN

        ps = [ctx.enter_context(nc.psum_tensor(f"ps{k}", [P, 512], F32)) for k in range(8)]

        w_ada, w_fin, w_in = a["w_ada"][0], a["w_ada_final"], a["w_in"][0]

        def cols(w, j):
            return w.rearrange("(p c) n -> p c n", c=KC)[:, :, j * 512:(j + 1) * 512]

        PROJ = ["u", "f", "q", "i", "g"]
        WCOL = {"q": 0, "f": 1, "i": 2, "g": 3, "u": 4}
        ADA = [(v, h) for v in (0, 1) for h in (0, 1)]
        ADA2 = [(v, h) for v in (2, 3, 4, 5, 6, 7) for h in (0, 1)]
        ADA_S5, ADA_HGRN, ADA_ROUTER = ADA2[:6], ADA2[6:8], ADA2[8:]

        def ada_cols(v, h):
            return cols(w_ada, 2 * v + h) if v < 6 else cols(w_fin, 2 * (v - 6) + h)

        wg, wu, wd = a["moe_w_gate"][0], a["moe_w_up"][0], a["moe_w_down"][0]
        pieces = [ada_cols(v, h) for v, h in ADA]
        pieces += [cols(w_in, WCOL[k]) for k in PROJ[:3]]
        pieces += [ada_cols(v, h) for v, h in ADA_S5]
        pieces += [cols(w_in, WCOL[k]) for k in PROJ[3:]]
        pieces += [ada_cols(v, h) for v, h in ADA_HGRN]
        GLU_PIECE = len(pieces)
        pieces += ["glu"]
        pieces += [a["w_out"][0].rearrange("(c p) n -> p c n", p=P)[:, :, j * 512:(j + 1) * 512] for j in range(2)]
        pieces += [ada_cols(v, h) for v, h in ADA_ROUTER]
        N0 = len(pieces)
        assert N0 % 4 == 0

        h2_sem = [sem(f"h2_rows_out{k}") for k in range(2)]
        fin_in = [sem(f"y_rows_in{t}") for t in range(TILES)]
        landed = [sem(f"piece_landed{k}") for k in range(SLOTS)]

        SMALL = 3

        def u_offset(r, q, s):
            return uT[32 * q:32 * q + 32, r, :].rearrange("p (c a s) -> p s a c", a=2, s=4)[:, s]

        S = {n: sem(n) for n in (
            "lgT_mm", "lgT_out", "y0_scaled", "xr_last_in", "gated", "identity", "fin_stored", "bc_g2", "q_ready", "cmask", "oml", "s5_ca", "ada_stored", "bc_g1", "bc_h2", "bc_fin",
            "c_in", "prm_in", "x_in", "bc_in", "small_in", "const", "const_step",
            "ada_mm", "ada_out", "csig", "cact", "ssq", "ms", "rms", "xn_ready",
            "tr_h", "h_dve", "h_act", "mod1", "act_step", "dve_step",
            "prm_exp", "prm_dve", "bc_tr", "bc_out", "proj_mm", "proj_act", "proj_dve",
            "s5_mat", "s5_tr", "s5_trout", "s5_T", "s5_Tout", "s5_U", "s5_W", "s5_X", "s5_Y", "s5_Yout", "s5_gin", "s5_g",
            "s5_fintr", "s5_finout",
            "lf", "cum_ready", "e_ready", "hprep", "kh_tr", "kh_out",
            "sc_mm", "sc_mask", "o_mm", "u_mm", "s_upd", "o_sq", "o_ms", "o_rms", "o_norm", "mix_tr", "mix_out",
            "s0_in", "vm_ready", "s0_new", "s0_out", "us_mm", "hs_out", "mod3", "ss_init", "s5_D", "s5_Up", "iota", "late_in",
            "glu_mm", "glu_sig", "glu_sq", "glu_ss", "glu_rt", "glu_mix",
            "xr_in", "wo_mm", "wo_t", "x2", "x2_sq", "x2_ms", "x2_rt", "xn2_ready", "tr2", "h2_dve", "h2_act",
            "lg_mm", "rt_exp", "rt_exp2", "acc_zero",
            "gu_mm", "g_sig", "act_ready", "at_mm", "at_out", "y_mm", "y_acc", "gs_mul", "flag", "pos", "tab0", "tab_set", "ix_in", "lg_read", "rank_mm", "SM_ready", "before", "xg0", "xg1", "xt_mm", "xt_act", "xt_dve", "ys0", "ys1", "yb_act", "yb_dve", "comb2", "xg_init",
            "x3", "x3_sq", "x3_ms", "x3_rt", "y_ready", "written")}

        def used_up(n):
            if n < 4:
                return S["ada_mm"], 2 + n + 1
            if n < 7:
                return S["proj_mm"], (4, 8, 12)[n - 4]
            if n < 13:
                return S["ada_mm"], 8 + (n - 7) + 1
            if n < 15:
                return S["proj_mm"], (17, 22)[n - 13]
            if n < GLU_PIECE:
                return S["ada_mm"], 14 + (n - 15) + 1
            if n < GLU_PIECE + 3:
                return (S["glu_mm"], SF) if n == GLU_PIECE else (S["wo_mm"], TILES)
            return S["ada_mm"], 16 + (n - GLU_PIECE - 3) + 1

        ada_dram = nc.dram_tensor("conditioning_rows", [8, 1, D], F32, kind="Internal").ap()
        ada_tok = nc.dram_tensor("conditioning_of_tokens", [8, NB, TS, D], F32, kind="Internal").ap()
        h2_dram = nc.dram_tensor("h2_rows", [NT, D], F32, kind="Internal").ap()
        y_dram = nc.dram_tensor("y_rows", [2 * NT, D], F32, kind="Internal").ap()
        tab_dram = nc.dram_tensor("token_of_row", [P * E, 1], I32, kind="Internal").ap()
        NOWHERE = 1 << 20

        block = ctx.enter_context(nc.Block())

        def store_rows(eng, v, done):
            q = 32 * (v % 4)
            eng.dma_start(ada_dram[v], rows8[q:q + 1, v // 4, :]).then_inc(done, 16)
            eng.dma_start(ada_tok[v], sb[q + 1:q + C9, ROWS8 + D * (v // 4):ROWS8 + D * (v // 4 + 1)].unsqueeze(1)
                          .to_broadcast([NB, TS, D])).then_inc(done, 16)

        def token_rows(eng, v, dst, done):
            eng.dma_start(dst[:, 0, :], ada_dram[v].to_broadcast([P, D])).then_inc(done, 16)
            eng.dma_start(dst[0:NS, 1, :], ada_tok[v].rearrange("b t d -> (b t) d")).then_inc(done, 16)

        @block.sync
        def _(sp):
            gsrc = wg.rearrange("g e (p c) f -> (g e) p (c f)", c=KC)
            usrc = wu.rearrange("g e (p c) f -> (g e) p (c f)", c=KC)
            dsrc = wd.rearrange("g e (p c) n -> (g e) p (c n)", c=2)

            def expert_piece(i, k):
                half, kind = divmod(k, 3)
                for b in range(2):
                    e = i * 4 + (2 * half + (kind if kind < 2 else b))
                    src = (gsrc, usrc)[b] if kind < 2 else dsrc
                    src = src[bass.ds(e, 1)].rearrange("o p n -> (o p) n")
                    sp.dma_start(slot[k][:, b * SLOT // 2:(b + 1) * SLOT // 2], src).then_inc(landed[k], 16)

            sp.dma_start(c9[0:1, :], a["c_prompt"]).then_inc(S["c_in"], 16)
            sp.dma_start(sb[1:C9, C9IN:C9IN + D], a["c_sample"]).then_inc(S["c_in"], 16)

            for n in range(N0):
                if n == 1:
                    sp.wait_ge(S["prm_in"], 16 * 10)
                if n >= 4:
                    sp.wait_ge(*used_up(n - 4))
                if n == GLU_PIECE:
                    dst = slot[n % 4][:, 0:4 * DH].rearrange("p (c n) -> p c n", c=4)
                    src = a["ssm_w_glu"][0].rearrange("(c p) n -> p c n", p=P)
                else:
                    dst, src = slot[n % 4].rearrange("p (c n) -> p c n", c=KC), pieces[n]
                sp.dma_start(dst, src).then_inc(landed[n % 4], 16)
                if n == 1:
                    for t in range(TILES):
                        src = a["x_prompt"][0, t * P:(t + 1) * P, :] if t < PT else a["x_sample"].rearrange("b t d -> (b t) d")
                        sp.dma_start(xin[0:ROWS[t], t, :], src).then_inc(S["x_in"], 16)
                if n == GLU_PIECE + 2:
                    sp.wait_ge(S["hs_out"], 16)
                    sp.wait_ge(S["s0_out"], 32)
                    sp.wait_ge(S["mix_tr"], TILES)
                    expert_piece(0, 4)
                    expert_piece(0, 5)
            for k in range(4):
                sp.wait_ge(*used_up(N0 - 4 + k))
                expert_piece(0, k)
            def more_pieces(units):
                with sp.Fori(1, E // 4) as i:
                    for k in range(6):
                        if k in (2, 5):
                            sp.wait_ge(S["y_mm"], i * 4 * units + 2 * units * (k // 3 - 1))
                        else:
                            sp.wait_ge(S["gu_mm"], i * 4 * units + units * ((0, 1, 0, 2, 3)[k] - 3))
                        expert_piece(i, k)

            sp.wait_ge(S["ada_out"], 20)
            for v in (6, 7):
                store_rows(sp, v, S["fin_stored"])
            sp.wait_ge(S["fin_stored"], 16 * 4)
            sp.wait_ge(S["xn2_ready"], TILES)
            token_rows(sp, 6, sfb, S["bc_fin"])
            token_rows(sp, 7, cfb, S["bc_fin"])
            sp.wait_ge(S["flag"], 1)
            dense = sp.value_load(flag[0:1, :].bitcast(I32), min_val=0, max_val=1)
            with sp.If(dense > 0):
                more_pieces(TILES)
            with sp.Else():
                more_pieces(1)

        @block.gpsimd
        def _(pool):
            n = [0]

            def step(ins):
                n[0] += 1
                ins.then_inc(S["const_step"], 1)
                pool.wait_ge(S["const_step"], n[0])

            pool.memset(ss, 1.0).then_inc(S["ss_init"], 1)
            step(pool.memset(ident, 0.0))
            pool.affine_select(out=ident, in_=ident, compare_op=ALU.not_equal, fill=1.0, base=0,
                               pattern=[[-1, P]], channel_multiplier=1).then_inc(S["identity"], 1)
            pool.wait_ge(S["identity"], 1)

            step(pool.memset(ones, 1.0))
            step(pool.memset(maskP, 1.0))
            mp = maskP.rearrange("p (j t) -> p j t", t=CH)
            step(pool.affine_select(out=mp, in_=mp, compare_op=ALU.is_ge, fill=0.0, base=0,
                                    pattern=[[CH, P // CH], [1, CH]], channel_multiplier=-1))
            step(pool.affine_select(out=mp, in_=mp, compare_op=ALU.is_ge, fill=0.0, base=0,
                                    pattern=[[-CH, P // CH], [0, CH]], channel_multiplier=1))
            step(pool.memset(maskS, 1.0))
            ms = maskS.rearrange("p (j t) -> p j t", t=TS)
            step(pool.affine_select(out=ms, in_=ms, compare_op=ALU.is_ge, fill=0.0, base=0,
                                    pattern=[[TS, NB], [1, TS]], channel_multiplier=-1))
            step(pool.affine_select(out=ms, in_=ms, compare_op=ALU.is_ge, fill=0.0, base=0,
                                    pattern=[[-TS, NB], [0, TS]], channel_multiplier=1))
            step(pool.memset(seqm, 1.0))
            step(pool.affine_select(out=seqm, in_=seqm, compare_op=ALU.is_ge, fill=0.0, base=0,
                                    pattern=[[-TS, NB]], channel_multiplier=1))
            pool.affine_select(out=seqm, in_=seqm, compare_op=ALU.is_ge, fill=0.0, base=TS - 1,
                               pattern=[[TS, NB]], channel_multiplier=-1).then_inc(S["const"], 1)
            pool.wait_ge(S["tr_h"], 2 * TILES)
            step(pool.memset(cmask, 1.0))
            step(pool.memset(cmask[:, 0:TP:CH], 0.0))
            pool.memset(cmask[:, TP:NT:TS], 0.0).then_inc(S["cmask"], 1)
            pool.wait_ge(S["cmask"], 1)
            for r in range(SF):
                if r == 0:
                    pool.wait_ge(S["proj_act"], 4)
                else:
                    pool.wait_ge(S["s5_Y"], 2 * r)

                for s in (2, 3):
                    for q in range(4):
                        ins = pool.tensor_copy(Um[32 * s:32 * s + 32, q], u_offset(r, q, s))
                ins.then_inc(S["s5_Up"], 1)
                pool.wait_ge(S["s5_Up"], r + 1)
                if r == 1:
                    for m in range(H):
                        pool.wait_ge(S["proj_act"], 9 + m)
                        pool.tensor_tensor(qT[:, m, :], qT[:, m, :], qraw, ALU.mult).then_inc(S["q_ready"], 1)
                        pool.wait_ge(S["q_ready"], m + 1)
            pool.wait_ge(S["ada_out"], 16)
            for v in (2, 3, 4, 5):
                store_rows(pool, v, S["ada_stored"])
            pool.wait_ge(S["late_in"], 16 * (2 + NG))
            step(pool.iota(iota_i.bitcast(mybir.dt.int32), pattern=[[1, E]], base=0, channel_multiplier=0))
            pool.tensor_copy(iota, iota_i.bitcast(mybir.dt.int32)).then_inc(S["iota"], 1)
            pool.tensor_copy(wrc[:, :, 0:NG], wgrp)
            for g in range(NG):
                ins = pool.tensor_copy(wrc[:, :, NG + NE * g:NG + NE * (g + 1)], wrt[:, g])
            ins.then_inc(S["iota"], 1)

            step(pool.iota(tokid.bitcast(I32), pattern=[[P, TILES]], base=0, channel_multiplier=1))
            pool.tensor_copy(pcol, tokid.bitcast(I32)[:, 0:1]).then_inc(S["iota"], 1)
            step(pool.iota(xix.bitcast(I32), pattern=[[0, E]], base=NOWHERE, channel_multiplier=0))
            pool.dma_start(tab_dram.rearrange("(p e) o -> p (e o)", e=E), xix.bitcast(I32)).then_inc(S["tab0"], 16)
            pool.wait_ge(S["sc_mask"], TILES)
            step(pool.memset(before, 1.0))
            pool.affine_select(out=before, in_=before, compare_op=ALU.is_gt, fill=0.0, base=0,
                               pattern=[[1, P]], channel_multiplier=-1).then_inc(S["before"], 1)



            pool.wait_ge(S["flag"], 1)
            dense = pool.value_load(flag[0:1, :].bitcast(I32), min_val=0, max_val=1)
            with pool.If(dense > 0):
                pool.wait_ge(S["tab0"], 16)
            with pool.Else():
                def at_rows(t_ap):
                    return bass.IndirectOffsetOnAxis(ap=t_ap.bitcast(U32), axis=0)

                pool.wait_ge(S["h2_dve"], TILES)
                pool.wait_ge(S["tr2"], 2 * TILES)
                pool.wait_ge(h2_sem[0], 16 * 3)
                pool.wait_ge(h2_sem[1], 16 * 2)
                for k in range(2):
                    ins = pool.memset(xg[k], 0.0)
                ins.then_inc(S["xg_init"], 1)
                pool.wait_ge(S["xg_init"], 1)
                pool.wait_ge(S["pos"], 2)
                pool.wait_ge(S["tab0"], 16)
                for t in range(TILES):
                    for k in range(2):
                        pool.indirect_dma_start(out=tab_dram, out_offset=at_rows(pos[k][0:ROWS[t], t:t + 1]),
                                                in_=tokid[0:ROWS[t], t:t + 1].bitcast(I32), in_offset=None,
                                                bounds_check=P * E - 1, oob_is_err=False).then_inc(S["tab_set"], 16)
                pool.wait_ge(S["tab_set"], 16 * 2 * TILES)
                pool.dma_start(xix.bitcast(I32), tab_dram.rearrange("(p e) o -> p (e o)", e=E)).then_inc(S["ix_in"], 16)
                pool.wait_ge(S["ix_in"], 16)

                def gather(e):
                    pool.indirect_dma_start(out=xg[e % 2], out_offset=None, in_=h2_dram,
                                            in_offset=at_rows(xix[:, e:e + 1]), bounds_check=NT - 1,
                                            oob_is_err=False).then_inc(S[f"xg{e % 2}"], 16)

                gather(0)
                gather(1)
                pool.wait_ge(S["pos"], 5)
                for e in range(-2, E):
                    if e + 4 < E:
                        pool.wait_ge(S["xt_mm"], 2 * (e + 2) + 2)
                        gather(e + 4)
                    if e < 0:
                        continue
                    pool.wait_ge(S["yb_act"], e + 1)
                    pool.wait_ge(S["yb_dve"], e + 1)
                    pool.indirect_dma_start(out=y_dram, out_offset=at_rows(yix[:, e:e + 1]), in_=yb[e % 2], in_offset=None,
                                            bounds_check=2 * NT - 1, oob_is_err=False).then_inc(S[f"ys{e % 2}"], 16)
                for k in range(2):
                    pool.wait_ge(S[f"ys{k}"], 16 * (E // 2))
                for t in range(TILES):
                    for k in range(2):
                        dst = (acc[:, t, :], y1[t])[k][0:ROWS[t], :]
                        pool.indirect_dma_start(out=dst, out_offset=None, in_=y_dram,
                                                in_offset=at_rows(ypos[k][0:ROWS[t], t:t + 1]), bounds_check=2 * NT - 1,
                                                oob_is_err=False).then_inc(fin_in[t], 16)

        @block.scalar
        def _(act):
            n = [0]

            def step(ins):
                n[0] += 1
                ins.then_inc(S["act_step"], 1)
                act.wait_ge(S["act_step"], n[0])



            def load_rows(r0, n_, src):
                act.dma_start(sb[r0:r0 + n_, prow_off:prow_off + P], src).then_inc(S["prm_in"], 16)

            prow_off = PROW
            load_rows(0, 8, a["hgrn_lb_logits"].rearrange("l (h p) -> (l h) p", p=P))
            load_rows(8, 4, a["ssm_b_glu"].rearrange("l (h p) -> (l h) p", p=P))
            load_rows(12, 4, a["ssm_norm"].rearrange("l (h p) -> (l h) p", p=P))
            for k, name in enumerate(("ssm_a_re", "ssm_a_im", "ssm_log_dt")):
                load_rows(16 + 16 * k, NPAIR, a[name][0].rearrange("(r g) p -> r (g p)", g=2))
            act.dma_start(sb[64:80, prow_off:prow_off + P].rearrange("p (s q) -> p s q", s=4),
                          a["ssm_d"][0].rearrange("(r g) h -> r (g h)", g=2).unsqueeze(1)
                          .to_broadcast([NPAIR, 4, 2 * GH])).then_inc(S["prm_in"], 16)
            act.dma_start(gmixT, a["norm_mix"][0].rearrange("(p c) -> p c", c=KC)).then_inc(S["prm_in"], 16)
            act.dma_start(bias16[0:12, :], a["b_ada"].rearrange("l (j n) -> (l j) n", n=512)).then_inc(S["prm_in"], 16)
            act.dma_start(sb[12:16, BIAS:BIAS + 512],
                          a["b_ada_final"].rearrange("(j n) -> j n", n=512)).then_inc(S["prm_in"], 16)
            act.wait_ge(S["c_in"], 32)
            act.activation(c9s, c9, ACT.Sigmoid).then_inc(S["csig"], 1)
            ada_n = [0]

            def ada_wait():
                ada_n[0] += 1
                act.wait_ge(S["ada_mm"], ada_n[0])
                return ps[(ada_n[0] - 1) % 2]

            b = ada_wait()
            act.copy(cT, b[:, 0:KC * C9].rearrange("p (c r) -> p c r", c=KC)).then_inc(S["ada_out"], 1)
            b = ada_wait()
            act.copy(prm, b[:, 0:PARAMS]).then_inc(S["ada_out"], 1)

            act.wait_ge(S["ada_out"], 2)
            act.activation(par[0], prm[:, 48:64], ACT.Exp).then_inc(S["prm_exp"], 1)
            act.wait_ge(S["prm_dve"], 1)
            act.activation(par[2], par[1], ACT.Exp).then_inc(S["prm_exp"], 1)
            act.activation(par[3], par[1], ACT.Exp, scale=float(L)).then_inc(S["prm_exp"], 1)
            act.activation(lb, par[4][:, 0:H], ACT.Exp).then_inc(S["prm_exp"], 1)
            act.activation(oml, par[4][:, H:2 * H], ACT.Exp).then_inc(S["prm_exp"], 1)
            act.wait_ge(S["prm_dve"], 2)
            act.activation(par[5], par[6], ACT.Sin).then_inc(S["prm_exp"], 1)
            act.activation(par[7], par[8], ACT.Sin).then_inc(S["prm_exp"], 1)

            def ada_row(v, h):
                bank = ada_wait()
                r = 32 * (v % 4)
                act.copy(rows8[r:r + C9, v // 4, h * 512:(h + 1) * 512], bank[r:r + C9, :]).then_inc(S["ada_out"], 1)

            def ada_col(v):
                bank = ada_wait()
                act.copy(adaT[:, v], bank[:, 0:KC * C9].rearrange("p (c r) -> p c r", c=KC)).then_inc(S["ada_out"], 1)

            for k, name in enumerate(("ssm_b_re", "ssm_b_im")):
                act.dma_start(bin_[k], a[name][0].rearrange("g p h -> (g p) h").rearrange("(r q) h -> q r h", q=P))\
                   .then_inc(S["bc_in"], 16)
            for k, name in enumerate(("ssm_c_re", "ssm_c_im")):
                src = a[name][0].rearrange("(r g) h p -> r h g p", g=2)
                for half in range(2):
                    for g in range(2):
                        act.dma_start(crow[:, 2 * k + half, g * NP:(g + 1) * NP],
                                      src[8 * half:8 * half + 8, :, g, :]).then_inc(S["bc_in"], 16)
            for k, name in enumerate(("state_ssm_re", "state_ssm_im")):
                act.dma_start(xrow[:, k, :], a[name][0].rearrange("b (r g) p -> (b r) (g p)", g=2)).then_inc(S["bc_in"], 16)
            act.dma_start(ghg, a["hgrn_norm"].to_broadcast([P, DH])).then_inc(S["small_in"], 16)
            act.dma_start(brt[:, 0:NG], a["moe_b_group"].to_broadcast([P, NG])).then_inc(S["small_in"], 16)
            act.dma_start(brt[:, NG:], a["moe_b_router"].rearrange("l g e -> l (g e)").to_broadcast([P, E])).then_inc(S["small_in"], 16)



            for v, h in ADA:
                ada_row(v, h)
                if (v, h) == ADA[0]:
                    act.wait_ge(S["x_in"], 16 * TILES)
                    act.wait_ge(S["ss_init"], 1)
                    for t in range(TILES):
                        act.activation(junk[0:ROWS[t], :], xin[0:ROWS[t], t, :], ACT.Square,
                                       accum_out=ss[0:ROWS[t], t:t + 1]).then_inc(S["ssq"], 1)
                        act.wait_ge(S["ssq"], t + 1)
                    act.wait_ge(S["ms"], 1)
                    act.activation(rs[:, 0:TILES], ss[:, 0:TILES], ACT.Sqrt).then_inc(S["rms"], 1)
            ada_col(0)
            ada_col(1)



            act.wait_ge(S["mod1"], 1)
            for t in range(PT):
                act.wait_ge(S["tr_h"], 2 * t + 2)
                bank = ps[3 + 2 * (t % 2)].rearrange("p (c t) -> p c t", c=4)
                for c in range(4):
                    ins = act.activation(hT[:, 4 + c, t * P:(t + 1) * P], bank[:, c, :], ACT.Identity,
                                         bias=adaT[:, 0, 4 + c, 0:1], scale=A1[:, 4 + c, 0:1])
                ins.then_inc(S["h_act"], 1)

            def proj_cols(unit):
                b0, b1 = (ps[2 + 2 * (unit % 3)], ps[3 + 2 * (unit % 3)]) if unit < 4 else (ps[0], ps[1])
                act.wait_ge(S["proj_mm"], unit + 1)
                dst = (uT, fT, qT)[unit // 4][:, unit % 4]
                fn = ACT.Copy if unit < 4 else ACT.Sigmoid
                act.activation(dst[:, 0:TP], b0[:, :], fn)
                ins = act.activation(dst[:, TP:NT], b1[:, 0:NS], fn)
                if unit >= 8:
                    if unit > 8:
                        act.wait_ge(S["q_ready"], unit - 8)
                    act.activation(qraw[:, 0:TP], b0[:, :], ACT.Copy, scale=float(P) ** -0.5)
                    ins = act.activation(qraw[:, TP:NT], b1[:, 0:NS], ACT.Copy, scale=float(P) ** -0.5)
                ins.then_inc(S["proj_act"], 1)

            def proj_rows(unit):
                t, r = (unit - 12) % TILES, ROWS[(unit - 12) % TILES]
                act.wait_ge(S["proj_mm"], unit + 1)
                act.activation((V if unit < 17 else Gt)[0:r, t, :], ps[4 + unit % 4][0:r, :],
                               ACT.Copy if unit < 17 else ACT.Sigmoid).then_inc(S["proj_act"], 1)

            for unit in range(4):
                proj_cols(unit)

            for k in range(2):
                act.wait_ge(S["bc_tr"], 2)
                act.copy(CT[k].rearrange("p r h -> p (r h)"), ps[6][:, 256 * k:256 * k + 256]).then_inc(S["bc_out"], 1)
            for k in range(2):
                act.wait_ge(S["bc_tr"], 4)
                act.copy(X0[k].rearrange("p b r -> p (b r)"), ps[7][:, P * k:P * k + P]).then_inc(S["bc_out"], 1)

            beside = [(4, 5), (6, 7), (8, 9), (10, 11), ADA_S5[0:2], ADA_S5[2:3], ADA_S5[3:5], ADA_S5[5:6]]

            def beside_s5(j):
                for w in beside[j]:
                    ada_row(*w) if j >= 4 else proj_cols(w)

            for r in range(SF):
                beside_s5(2 * r)
                for k in range(2):
                    for hf in range(2):
                        m = 4 * r + 2 * k + hf
                        act.wait_ge(S["s5_tr"], m + 1)
                        act.copy(Bl[k][:, 2 * hf:2 * hf + 2].rearrange("p q a n -> p (q a n)"), ps[2 + 2 * k + hf][:, :])\
                           .then_inc(S["s5_trout"], 1)
                for hf in range(2):
                    act.wait_ge(S["s5_T"], 2 * r + hf + 1)
                    for s in range(4):
                        w = 2 * P - 32 * s
                        act.copy(Tm[32 * s:32 * s + 32, 2 * hf:2 * hf + 2, 32 * s:],
                                 ps[6 + hf][0:32, :].rearrange("p (q n) -> p q n", q=2)[:, :, 0:w]).then_inc(S["s5_Tout"], 1)
                beside_s5(2 * r + 1)
                for hf in range(2):
                    act.wait_ge(S["s5_Y"], 2 * r + hf + 1)
                    for q in range(2):
                        for t in range(4):
                            dst = uT[64 * hf + 32 * q:64 * hf + 32 * q + 32, r, :].rearrange("p (c b t) -> p t b c", b=2, t=4)[:, t]
                            act.copy(dst, ps[4 + hf][32 * t:32 * t + 32, 144 * q:144 * q + 144]
                                     .rearrange("p (b c) -> p b c", b=2)).then_inc(S["s5_Yout"], 1)
                act.wait_ge(S["s5_gin"], r + 1)
                act.activation(at(tq[1], NT), at(tq[0], NT), ACT.Sigmoid, scale=1.5957691216057308).then_inc(S["s5_g"], 1)

            act.wait_ge(S["s5_g"], SF)
            for k in range(2):
                act.wait_ge(S["s5_fintr"], k + 1)
                act.copy(at(tq[0] + 256 * k, P), ps[2 + k][:, 0:P])
                act.copy(at(tq[0] + 256 * k + P, P, NPAIR), ps[2 + k][0:NPAIR, P:2 * P]).then_inc(S["s5_finout"], 1)
            act.wait_ge(S["s5_finout"], 2)
            act.wait_ge(S["s5_X"], SF)
            for k in range(2):
                act.dma_start(o[("ssm_re_sample", "ssm_im_sample")[k]][0].rearrange("b (r g) p -> (b r) (g p)", g=2),
                              at(tq[0] + 256 * k, P)).then_inc(S["written"], 16)
                act.dma_start(o[("ssm_re_prompt", "ssm_im_prompt")[k]][0, 0].rearrange("(r g) p -> r (g p)", g=2),
                              at(tq[0] + 256 * k + P, P, NPAIR)).then_inc(S["written"], 16)

            for h in range(H):
                if h >= 1:
                    act.wait_ge(S["hprep"], h)
                act.wait_ge(S["oml"], 1)
                act.activation(d1, fT[:, h, :], ACT.Ln, scale=oml[:, h:h + 1], bias=lb[:, h:h + 1]).then_inc(S["lf"], 1)
                act.wait_ge(S["cum_ready"], h + 1)
                act.activation(Ex, cum, ACT.Exp).then_inc(S["e_ready"], 1)
                act.activation(d2, d2, ACT.Exp, scale=-1.0).then_inc(S["e_ready"], 1)
                act.wait_ge(S["e_ready"], 4 * h + 1)
                act.activation(cum, d1, ACT.Exp).then_inc(S["e_ready"], 1)
                act.wait_ge(S["e_ready"], 4 * h + 3)
                act.activation(d1, d1, ACT.Exp, scale=-1.0).then_inc(S["e_ready"], 1)
                for unit in (12, 13, 14) if h < 3 else (12,):
                    proj_rows(unit + 3 * h)
                if h == 3:
                    for w in ADA_HGRN:
                        ada_row(*w)
                act.wait_ge(S["kh_tr"], h + 1)
                act.copy(KhT[:, 0:PT, h * P:(h + 1) * P], ps[2][:, :].rearrange("p (t n) -> p t n", t=PT))
                act.copy(KhT[0:NS, PT, h * P:(h + 1) * P], ps[3][0:NS, 0:P]).then_inc(S["kh_out"], 1)

            act.wait_ge(S["hprep"], H)
            act.wait_ge(S["kh_tr"], H)

            def load_s0(half):
                act.dma_start(S0[half].rearrange("k b h v -> k (b h) v"),
                              a["state_hgrn"][0, 4 * half:4 * half + 4].rearrange("b h k v -> k (b h) v"))\
                   .then_inc(S["s0_in"], 16)

            load_s0(0)
            load_s0(1)
            for t in range(TILES):
                r = ROWS[t]
                if t == 0:
                    act.wait_ge(S["written"], 64)
                if t == PT:
                    act.wait_ge(S["s_upd"], NCH)
                    act.dma_start(o["hgrn_prompt"][0, 0].rearrange("h k v -> k h v"), Sr[NCH % 3]).then_inc(S["hs_out"], 16)
                    for half in range(2):
                        act.wait_ge(S["s0_new"], half + 1)
                        act.dma_start(o["hgrn_sample"][0, 4 * half:4 * half + 4].rearrange("b h k v -> k (b h) v"),
                                      S0[half].rearrange("k b h v -> k (b h) v")).then_inc(S["s0_out"], 16)
                act.wait_ge(S["o_mm"], t + 1)
                ob = ps[4 + t % 2].rearrange("p (h v) -> p h v", h=H)
                for h in range(H):
                    ins = act.activation(sq1[0:r, :], ob[0:r, h, :], ACT.Square, accum_out=ss[0:r, h:h + 1])
                    if h < H - 1:
                        step(ins)
                ins.then_inc(S["o_sq"], 1)
                act.wait_ge(S["o_ms"], t + 1)
                act.activation(rs[0:r, 0:H], ss[0:r, 0:H], ACT.Sqrt).then_inc(S["o_rms"], 1)
                act.wait_ge(S["mix_tr"], t + 1)
                act.copy(mixT[:, 0:H, t * P:t * P + r], ps[3].rearrange("p (c t) -> p c t", c=H)[:, :, 0:r])\
                   .then_inc(S["mix_out"], 1)

            act.wait_ge(S["s0_out"], 32)
            act.dma_start(gfin, a["norm_final"].unsqueeze(0).to_broadcast([P, D])).then_inc(S["late_in"], 16)
            act.dma_start(wgrp, a["moe_w_group"][0].rearrange("(p c) g -> p c g", c=KC)).then_inc(S["late_in"], 16)
            for g in range(NG):
                act.dma_start(wrt[:, g], a["moe_w_router"][0, g].rearrange("(p c) e -> p c e", c=KC)).then_inc(S["late_in"], 16)

            def load_x(t):
                src = a["x_prompt"][0, t * P:(t + 1) * P, :] if t < PT else a["x_sample"].rearrange("b t d -> (b t) d")
                act.dma_start(x[0:ROWS[t], t, :], src).then_inc(S["xr_in" if t < PT else "xr_last_in"], 16)

            act.wait_ge(S["ada_stored"], 128)
            act.wait_ge(S["o_norm"], TILES)
            token_rows(act, 2, g1b, S["bc_g1"])
            for t in range(PT):
                load_x(t)
            act.dma_start(gffn, a["norm_ffn"].to_broadcast([P, D])).then_inc(S["bc_h2"], 16)

            for m in range(SF):
                act.wait_ge(S["glu_mm"], m + 1)
                act.activation(y2[:, m, 0:TP], ps[2 + 2 * (m % 2)][:, :], ACT.Sigmoid, bias=prm[:, 8 + m:9 + m])
                act.activation(y2[:, m, TP:NT], ps[3 + 2 * (m % 2)][:, 0:NS], ACT.Sigmoid, bias=prm[:, 8 + m:9 + m])\
                   .then_inc(S["glu_sig"], 1)
            act.wait_ge(S["glu_rt"], 1)
            act.activation(rsy, rsy, ACT.Sqrt).then_inc(S["glu_rt"], 1)

            act.wait_ge(S["glu_mix"], 1)
            token_rows(act, 4, A2b, S["bc_h2"])
            token_rows(act, 3, B2b, S["bc_h2"])
            load_x(PT)
            token_rows(act, 5, g2b, S["bc_g2"])

            def late_row(v, h):
                act.wait_ge(S["ada_mm"], 17 + 2 * (v - 6) + h)
                r = 32 * (v % 4)
                act.copy(rows8[r:r + C9, v // 4, h * 512:(h + 1) * 512], ps[2 + h][r:r + C9, :]).then_inc(S["ada_out"], 1)

            for t in range(TILES):
                r = ROWS[t]
                act.wait_ge(S["x2"], t + 1)
                act.activation(xn2[t % 2][0:r, :], x[0:r, t, :], ACT.Square, accum_out=ss[0:r, t:t + 1])\
                   .then_inc(S["x2_sq"], 1)
                act.wait_ge(S["x2_ms"], t + 1)
                act.activation(rs[0:r, t:t + 1], ss[0:r, t:t + 1], ACT.Sqrt).then_inc(S["x2_rt"], 1)
                act.wait_ge(S["xn2_ready"], t + 1)
                act.dma_start(h2_dram[t * P:t * P + r, :], xn2[t % 2][0:r, :]).then_inc(h2_sem[t % 2], 16)
                if t == PT:
                    for v, h in ADA_ROUTER[:2]:
                        late_row(v, h)
                    act.wait_ge(S["lgT_mm"], 1)
                    act.copy(lgT[:, 0:TP], ps[0][0:LG, :]).then_inc(S["lgT_out"], 1)
                act.wait_ge(S["tr2"], 2 * t + 2)
                bank = ps[5 + 2 * (t % 2)].rearrange("p (c t) -> p c t", c=4)
                act.copy(h2T[:, 4:KC, t * P:t * P + r], bank[:, :, 0:r]).then_inc(S["h2_act"], 1)

            act.wait_ge(S["lgT_mm"], 2)
            act.copy(lgT[:, TP:NT], ps[1][0:LG, 0:NS]).then_inc(S["lgT_out"], 1)
            act.wait_ge(S["rt_exp"], 1)
            for t in range(TILES):
                step(act.activation(RT["ge"][:, t, :], RT["gl"][:, t, 0:NG], ACT.Exp, bias=RT["ngm"][:, t:t + 1],
                                    accum_out=RT["gs"][:, t:t + 1]))
            for v, h in ADA_ROUTER[2:]:
                late_row(v, h)
            act.wait_ge(S["rt_exp"], 2)
            act.activation(RT["e1"], RT["dv"], ACT.Exp).then_inc(S["rt_exp2"], 1)

            act.wait_ge(S["fin_stored"], 64)
            act.wait_ge(S["ada_stored"], 128)
            act.wait_ge(S["flag"], 1)
            dense = act.value_load(flag[0:1, :].bitcast(I32), min_val=0, max_val=1)
            with act.If(dense > 0):
                with act.Fori(0, E // 4) as i:
                    base = i * (4 * TILES)

                    def gate_sigmoid(k):
                        r = ROWS[k % TILES]
                        act.wait_ge(S["gu_mm"], base + (k + 1))
                        act.activation(sg[k % 2][0:r, :], ps[k % 2][0:r, 0:DE], ACT.Sigmoid).then_inc(S["g_sig"], 1)

                    gate_sigmoid(0)
                    for k in range(4 * TILES):
                        r = ROWS[k % TILES]
                        if k + 1 < 4 * TILES:
                            gate_sigmoid(k + 1)
                        act.wait_ge(S["at_mm"], base + (k + 1))
                        act.copy(aT[k % 2][:, :, 0:r], ps[2 + k % 2].rearrange("p (c t) -> p c t", c=4)[:, 0:2, 0:r])\
                           .then_inc(S["at_out"], 1)

            with act.Else():
                def turned(base, k):
                    act.wait_ge(S["xt_mm"], 2 * base + 2 * k + 2)
                    act.copy(xT[k % 2][:, 4:KC, :].rearrange("p c t -> p (c t)"), ps[1][:, :]).then_inc(S["xt_act"], 1)

                def gates(base, k):
                    act.wait_ge(S["gu_mm"], base + (k + 1))
                    act.activation(sg[k % 2], ps[2 + k % 2][:, 0:DE], ACT.Sigmoid).then_inc(S["g_sig"], 1)

                def four(base, first, last):
                    for k in range(4):
                        act.wait_ge(S["at_mm"], base + (k + 1))
                        act.copy(aT[k % 2].rearrange("p c t -> p (c t)"), ps[4][:, 0:2 * P] if k % 2 == 0 else ps[5][:, 0:2 * P])\
                           .then_inc(S["at_out"], 1)
                        if not (last and k == 3):
                            gates(base, k + 1)
                        if not (last and k >= 2):
                            turned(base, k + 2)
                        act.wait_ge(S["y_mm"], base + (k + 1))
                        if first and k < 2:
                            pass
                        else:
                            act.wait_ge(S[f"ys{k % 2}"], base * 8 + 16 * (k // 2))
                        act.copy(yb[k % 2][:, 0:512], ps[6][:, :]).then_inc(S["yb_act"], 1)

                turned(0, 0)
                gates(0, 0)
                turned(0, 1)
                four(0, True, False)
                with act.Fori(1, E // 4 - 1) as i:
                    four(i * 4, False, False)
                four(E - 4, False, True)
                for t in range(TILES):
                    r = ROWS[t]
                    act.wait_ge(fin_in[t], 32)
                    act.activation(acc[0:r, t, :], acc[0:r, t, :], ACT.Copy, scale=RT["w0"][0:r, t:t + 1])\
                        .then_inc(S["y0_scaled"], 1)

            for t in range(TILES):
                act.wait_ge(S["x3"], t + 1)
                r = ROWS[t]
                act.activation(acc[0:r, t, :], x[0:r, t, :], ACT.Square, accum_out=ss[0:r, t:t + 1])\
                   .then_inc(S["x3_sq"], 1)
            act.wait_ge(S["x3_ms"], 1)
            act.activation(rs[:, 0:TILES], ss[:, 0:TILES], ACT.Sqrt).then_inc(S["x3_rt"], 1)
            for t in range(TILES):
                act.wait_ge(S["y_ready"], t + 1)
                dst = o["y_prompt"][0, t * P:(t + 1) * P, :] if t < PT else o["y_sample"].rearrange("b t d -> (b t) d")
                act.dma_start(dst, x[0:ROWS[t], t, :]).then_inc(S["written"], 16)
            act.wait_ge(S["written"], 16 * (4 + TILES))


        @block.vector
        def _(dve):
            n = [0]

            def link(ins):
                n[0] += 1
                ins.then_inc(S["dve_step"], 1)
                dve.wait_ge(S["dve_step"], n[0])

            def tt(out, x0, x1, op):
                return dve.tensor_tensor(out, x0, x1, op)

            def cprod(t, ar, ai, br, bi):
                tt(t[0], ar, br, ALU.mult)
                tt(t[1], ai, bi, ALU.mult)
                tt(t[2], ar, bi, ALU.mult)
                link(tt(t[3], ai, br, ALU.mult))

            dve.wait_ge(S["csig"], 1)
            tt(c9, c9, c9s, ALU.mult).then_inc(S["cact"], 1)

            a_im = prm[:, 32:48]
            dve.wait_ge(S["ada_out"], 2)
            dve.tensor_scalar(par[9], prm[:, 16:32], -1e-4, None, ALU.min)
            link(tt(par[11][:, 0:H], prm[:, 0:H], prm[:, H:2 * H], ALU.max))
            tt(par[4][:, 0:H], prm[:, 0:H], par[11][:, 0:H], ALU.subtract)
            tt(par[4][:, H:2 * H], prm[:, H:2 * H], par[11][:, 0:H], ALU.subtract)
            dve.wait_ge(S["prm_exp"], 1)
            tt(par[10], a_im, par[0], ALU.mult)
            tt(par[1], par[9], par[0], ALU.mult).then_inc(S["prm_dve"], 1)
            MAGIC = 12582912.0
            dve.wait_ge(S["prm_dve"], 1)
            link(dve.tensor_scalar(par[12], par[10], 1.0 / (2 * PI), MAGIC, ALU.mult, ALU.add))
            link(dve.tensor_scalar(par[12], par[12], MAGIC, None, ALU.subtract))
            link(dve.scalar_tensor_tensor(out=par[8], in0=par[12], scalar=-6.28125, in1=par[10], op0=ALU.mult, op1=ALU.add))
            link(dve.scalar_tensor_tensor(out=par[8], in0=par[12], scalar=-(2 * PI - 6.28125), in1=par[8],
                                          op0=ALU.mult, op1=ALU.add))
            link(dve.tensor_scalar(par[13], par[8], PI / 2, -2 * PI, ALU.is_gt, ALU.mult))
            link(dve.scalar_tensor_tensor(out=par[6], in0=par[8], scalar=PI / 2, in1=par[13], op0=ALU.add, op1=ALU.add))
            LIM = 3.1415925
            dve.tensor_scalar(par[6], par[6], LIM, -LIM, ALU.min, ALU.max)
            dve.tensor_scalar(par[8], par[8], LIM, -LIM, ALU.min, ALU.max).then_inc(S["prm_dve"], 1)
            dve.wait_ge(S["prm_exp"], 7)
            link(tt(par[11][:, 0:H], lb, oml, ALU.add))
            link(dve.reciprocal(par[11][:, 0:H], par[11][:, 0:H]))
            link(tt(lb, lb, par[11][:, 0:H], ALU.mult))
            dve.tensor_scalar(noml, lb, -1.0, None, ALU.add)
            dve.tensor_scalar(oml, lb, -1.0, 1.0, ALU.mult, ALU.add).then_inc(S["oml"], 1)
            dve.memset(Pw[0][:, 0, :], 1.0)
            dve.memset(Pw[1][:, 0, :], 0.0)
            tt(Pw[0][:, 1, :], par[2], par[5], ALU.mult)
            link(tt(Pw[1][:, 1, :], par[2], par[7], ALU.mult))
            small = [par[k] for k in (14, 15, 16, 17)]
            cr, ci = par[18], par[19]
            src = (par[5], par[7])
            for _ in range(3):
                cprod(small, src[0], src[1], src[0], src[1])
                tt(cr, small[0], small[1], ALU.subtract)
                link(tt(ci, small[2], small[3], ALU.add))
                src = (cr, ci)
            dve.wait_ge(S["ssq"], TILES)
            dve.tensor_scalar(ss[:, 0:TILES], ss[:, 0:TILES], 1.0 / D, EPS, ALU.mult, ALU.add).then_inc(S["ms"], 1)
            dve.wait_ge(S["rms"], 1)
            link(dve.reciprocal(rs[:, 0:TILES], rs[:, 0:TILES]))
            for t in range(TILES):
                r = ROWS[t]
                dve.tensor_scalar(xin[0:r, t, :], xin[0:r, t, :], rs[0:r, t:t + 1], None, ALU.mult).then_inc(S["xn_ready"], 1)
            lre = par[9]
            tt(par[20], lre, lre, ALU.mult)
            tt(par[21], a_im, a_im, ALU.mult)
            link(dve.tensor_scalar(par[22], Pw[0][:, 1, :], 1.0, None, ALU.subtract))
            link(tt(par[20], par[20], par[21], ALU.add))
            link(dve.reciprocal(par[20], par[20]))
            tt(small[0], par[22], lre, ALU.mult)
            tt(small[1], Pw[1][:, 1, :], a_im, ALU.mult)
            tt(small[2], Pw[1][:, 1, :], lre, ALU.mult)
            link(tt(small[3], par[22], a_im, ALU.mult))
            tt(par[21], small[0], small[1], ALU.add)
            link(tt(par[23], small[2], small[3], ALU.subtract))
            tt(par[21], par[21], par[20], ALU.mult)
            link(tt(par[23], par[23], par[20], ALU.mult))
            dve.wait_ge(S["ada_out"], 8)
            dve.wait_ge(S["prm_in"], 16 * 10)
            dve.scalar_tensor_tensor(out=A1, in0=adaT[:, 1], scalar=1.0, in1=gmixT.unsqueeze(2).to_broadcast([P, KC, C9]),
                                     op0=ALU.add, op1=ALU.mult).then_inc(S["mod1"], 1)
            dve.wait_ge(S["mod1"], 1)

            def modulate(t, dst, A, v_, banks, bank_ready, done):
                if t < PT:
                    dve.wait_ge(bank_ready, 2 * t + 1)
                    bank = banks[0].rearrange("p (c t) -> p c t", c=4)
                    for c in range(4):
                        ins = dve.tensor_scalar(dst[:, c, t * P:(t + 1) * P], bank[:, c, :], A[:, c, 0:1],
                                                adaT[:, v_, c, 0:1], ALU.mult, ALU.add)
                else:
                    dve.wait_ge(bank_ready, 2 * t + 2)
                    for half in range(2):
                        bank = banks[half].rearrange("p (c t) -> p c t", c=4)[:, :, 0:NS]
                        cs = slice(4 * half, 4 * half + 4)
                        out = dst[:, cs, TP:NT].rearrange("p c (b t) -> p c b t", t=TS)
                        link(tt(out, bank.rearrange("p c (b t) -> p c b t", t=TS),
                                A[:, cs, 1:C9].unsqueeze(3).to_broadcast([P, 4, NB, TS]), ALU.mult))
                        ins = tt(out, out, adaT[:, v_, cs, 1:C9].unsqueeze(3).to_broadcast([P, 4, NB, TS]), ALU.add)
                ins.then_inc(done, 1)

            for t in range(TILES):
                modulate(t, hT, A1, 0, (ps[2 + 2 * (t % 2)], ps[3 + 2 * (t % 2)]), S["tr_h"], S["h_dve"])

            dve.wait_ge(S["bc_in"], 16 * 12)
            big = [at(t_, 256) for t_ in tq]
            v = [t_.rearrange("p (r h) -> p r h", h=GH) for t_ in big]
            kr, ki = (par[k].unsqueeze(2).to_broadcast([P, NPAIR, GH]) for k in (21, 23))
            cprod(v, kr, ki, bin_[0], bin_[1])
            tt(BB[0], v[0], v[1], ALU.subtract)
            link(tt(BB[1], v[2], v[3], ALU.add))

            def powers(X, r1, r2, idx, count, by):
                m_ = [at(t_, count * NPAIR).rearrange("p (j r) -> p j r", r=NPAIR) for t_ in tq]
                b_ = [z.unsqueeze(1).to_broadcast([P, count, NPAIR]) for z in by]
                cprod(m_, X[0][:, r1:r1 + count, :], X[1][:, r1:r1 + count, :], b_[0], b_[1])
                tt(X[0][:, idx:idx + count, :], m_[0], m_[1], ALU.subtract)
                link(tt(X[1][:, idx:idx + count, :], m_[2], m_[3], ALU.add))

            powers(Pw, 1, 0, 2, 1, (Pw[0][:, 1, :], Pw[1][:, 1, :]))
            powers(Pw, 1, 0, 3, 2, (Pw[0][:, 2, :], Pw[1][:, 2, :]))
            powers(Pw, 1, 0, 5, 4, (Pw[0][:, 4, :], Pw[1][:, 4, :]))
            for s in range(L):
                for k in range(2):
                    dve.tensor_copy(PwR[k][:, s, :], Pw[k][:, L - 1 - s, :])
            RT_ = [z.rearrange("p r c -> p c r") for z in R]
            dve.memset(RT_[0][:, 0, :], 1.0)
            dve.memset(RT_[1][:, 0, :], 0.0)
            dve.tensor_copy(RT_[0][:, 1, :], cr)
            link(dve.tensor_copy(RT_[1][:, 1, :], ci))
            m = 2
            while m < PC:
                cprod(small, RT_[0][:, m - 1, :], RT_[1][:, m - 1, :], cr, ci)
                tt(par[20], small[0], small[1], ALU.subtract)
                link(tt(par[22], small[2], small[3], ALU.add))
                powers(RT_, 0, 0, m, m, (par[20], par[22]))
                m *= 2

            dve.wait_ge(S["const"], 1)
            dve.wait_ge(S["small_in"], 16 * SMALL)
            dve.wait_ge(S["bc_out"], 4)
            dve.memset(at(V_, 2048), 0.0)
            dve.memset(at(EXT, 2304), 0.0)
            dve.memset(Tm, 0.0)
            dve.memset(Xb[0], 0.0)
            link(dve.memset(Xb[1], 0.0))
            def s5_out_matrices(r):
                sl = slice(4 * r, 4 * r + 4)
                t9 = [at(t_, 576).rearrange("p (q j h) -> p q j h", q=4, j=L + 1) for t_ in tq]
                c_ = [CT[k][:, sl, :].unsqueeze(2).to_broadcast([P, 4, L + 1, GH]) for k in range(2)]
                p_ = [Pw[k][:, :, sl].rearrange("p j r -> p r j").unsqueeze(3).to_broadcast([P, 4, L + 1, GH]) for k in range(2)]
                cprod(t9, c_[0], c_[1], p_[0], p_[1])
                for g in range(2):
                    w = slice(NP * g, NP * g + NP)
                    h_ = slice(GH * g, GH * g + GH)
                    tt(CA[0][w, :, :, h_], t9[0][w], t9[1][w], ALU.subtract)
                    ins = dve.scalar_tensor_tensor(out=CA[1][w, :, :, h_], in0=t9[2][w], scalar=-1.0, in1=t9[3][w],
                                                   op0=ALU.mult, op1=ALU.subtract)
                ins.then_inc(S["s5_ca"], 1)
                dve.wait_ge(S["s5_ca"], r + 1)

            def s5_in_matrices(r):
                sl = slice(4 * r, 4 * r + 4)
                t8 = [at(t_, 512).rearrange("p (q j h) -> p q j h", q=4, j=L) for t_ in tq]
                b_ = [BB[k][:, sl, :].unsqueeze(2).to_broadcast([P, 4, L, GH]) for k in range(2)]
                p_ = [PwR[k][:, :, sl].rearrange("p j r -> p r j").unsqueeze(3).to_broadcast([P, 4, L, GH]) for k in range(2)]
                cprod(t8, b_[0], b_[1], p_[0], p_[1])
                for g in range(2):
                    w = slice(NP * g, NP * g + NP)
                    h_ = slice(GH * g, GH * g + GH)
                    tt(AB[0][w, :, :, h_], t8[0][w], t8[1][w], ALU.subtract)
                    ins = tt(AB[1][w, :, :, h_], t8[2][w], t8[3][w], ALU.add)
                ins.then_inc(S["s5_mat"], 1)
                dve.wait_ge(S["s5_mat"], r + 1)

            s5_in_matrices(0)
            for r in range(SF):
                sl = slice(4 * r, 4 * r + 4)
                s5_out_matrices(r)
                dve.wait_ge(S["proj_act"], 4)
                for s in (0, 1):
                    for q in range(4):
                        ins = dve.tensor_copy(Um[32 * s:32 * s + 32, q], u_offset(r, q, s))
                ins.then_inc(S["s5_U"], 1)
                for k in range(2):
                    dve.tensor_copy(Xb[k][:, :, PC:NC], X0[k][:, :, sl].rearrange("p b r -> p r b"))
                dve.wait_ge(S["s5_Tout"], 8 * (r + 1))
                for q in range(4):
                    ins = dve.scalar_tensor_tensor(out=Tm[:, q, 0:P], in0=ident, scalar=prm[:, 64 + 4 * r + q:65 + 4 * r + q],
                                                   in1=Tm[:, q, 0:P], op0=ALU.mult, op1=ALU.add)
                ins.then_inc(S["s5_D"], 1)
                dve.wait_ge(S["s5_W"], r + 1)
                W = [ps[2 + k][:, 0:4 * NC].rearrange("p (q c) -> p q c", q=4) for k in range(2)]
                t4 = [at(t_, 4 * PC).rearrange("p (q c) -> p q c", q=4) for t_ in tq]
                Rr = [R[k][:, sl, :] for k in range(2)]
                cprod(t4, Rr[0], Rr[1], W[0][:, :, 0:PC], W[1][:, :, 0:PC])
                tt(Wp[0], t4[0], t4[1], ALU.add)
                link(tt(Wp[1], t4[2], t4[3], ALU.subtract))
                for k in range(2):
                    for q in range(4):
                        ins = dve.tensor_tensor_scan(Z_[k][:, q, :], par[3][:, 4 * r + q:4 * r + q + 1].to_broadcast([P, PC]),
                                                     Wp[k][:, q, :], 0.0, ALU.mult, ALU.add)
                link(ins)
                cprod(t4, Rr[0], Rr[1], Z_[0], Z_[1])
                for k in range(2):
                    op = (ALU.subtract, ALU.add)[k]
                    x0, x1 = t4[2 * k], t4[2 * k + 1]
                    tt(Xb[k][:, :, 1:PC], x0[:, :, 0:PC - 1], x1[:, :, 0:PC - 1], op)
                    ins = tt(fin[k][:, NB, sl], x0[:, :, PC - 1], x1[:, :, PC - 1], op)
                link(ins)
                t2 = [at(t_, NB * 4).rearrange("p (b q) -> p b q", b=NB) for t_ in tq]
                a8 = [Pw[k][:, L, sl].unsqueeze(1).to_broadcast([P, NB, 4]) for k in range(2)]
                cprod(t2, X0[0][:, :, sl], X0[1][:, :, sl], a8[0], a8[1])
                tt(t2[0], t2[0], t2[1], ALU.subtract)
                link(tt(t2[2], t2[2], t2[3], ALU.add))
                for k in range(2):
                    ins = tt(fin[k][:, 0:NB, sl], t2[2 * k], W[k][:, :, PC:NC].rearrange("p q b -> p b q"), ALU.add)
                ins.then_inc(S["s5_X"], 1)
                dve.wait_ge(S["s5_X"], r + 1)
                if r + 1 < SF:
                    s5_in_matrices(r + 1)
                dve.wait_ge(S["s5_Yout"], 16 * (r + 1))
                y = uT[:, r, :]
                link(tt(at(tq[0], NT), y, y, ALU.mult))
                link(dve.tensor_scalar(at(tq[0], NT), at(tq[0], NT), 0.044715, 1.0, ALU.mult, ALU.add))
                tt(at(tq[0], NT), at(tq[0], NT), y, ALU.mult).then_inc(S["s5_gin"], 1)
                dve.wait_ge(S["s5_g"], r + 1)
                link(tt(y, y, at(tq[1], NT), ALU.mult))

            def out_gate(t):
                unit, r = 17 + t, ROWS[t]
                dve.wait_ge(S["proj_act"], unit + 1)
                tt(Gt[0:r, t, :], ps[4 + unit % 4][0:r, :], Gt[0:r, t, :], ALU.mult).then_inc(S["proj_dve"], 1)
                dve.wait_ge(S["proj_dve"], 1 + t)
                link(tt(Gt[0:r, t, :], Gt[0:r, t, :], ghg[0:r, :], ALU.mult))

            dve.wait_ge(S["cmask"], 1)
            dve.wait_ge(S["q_ready"], H)
            for h in range(H):
                if h == 3:
                    out_gate(0)
                dve.wait_ge(S["lf"], h + 1)
                if h >= 1:
                    dve.wait_ge(S["kh_tr"], h)
                link(dve.tensor_tensor_scan(cum, cmask, d1, 0.0, ALU.mult, ALU.add))
                for c0, c1, w in ((0, TP, CH), (TP, NT, TS)):
                    cv, v1, v2_ = (z[:, c0:c1].rearrange("p (c t) -> p c t", t=w) for z in (cum, d1, d2))
                    shape = [P, (c1 - c0) // w, w]
                    tt(v1, cv, cv[:, :, w // 2 - 1:w // 2].to_broadcast(shape), ALU.subtract)
                    ins = tt(v2_, cv, cv[:, :, w - 1:w].to_broadcast(shape), ALU.subtract)
                ins.then_inc(S["cum_ready"], 1)
                link(dve.tensor_scalar(Kh, fT[:, h, :], noml[:, h:h + 1], oml[:, h:h + 1], ALU.mult, ALU.add))
                dve.wait_ge(S["e_ready"], 4 * (h + 1))
                dve.tensor_copy(dl[:, h, :], Ex[:, CH - 1:TP:CH])
                dve.tensor_copy(dls[:, h, :], Ex[:, TP + TS - 1:NT:TS])
                tt(Qt[:, h, :], qT[:, h, :], cum, ALU.mult)
                tt(fT[:, h, :], Kh, d1, ALU.mult)
                link(tt(qT[:, h, :], qT[:, h, :], Ex, ALU.mult))
                tt(Kh, Kh, d2, ALU.mult).then_inc(S["hprep"], 1)

            for t in range(1, TILES):
                out_gate(t)

            def mask(t):
                r = ROWS[t]
                dve.wait_ge(S["sc_mm"], t + 1)
                if t >= 2:
                    dve.wait_ge(S["o_mm"], t - 1)
                mk = (maskP if t < PT else maskS).unsqueeze(1).to_broadcast([r, H, r])
                tt(sT[t % 2][0:r, :, 0:r], ps[2][0:r, :].rearrange("p (h t) -> p h t", h=H)[:, :, 0:r], mk, ALU.mult)\
                    .then_inc(S["sc_mask"], 1)

            def norm_o(t):
                r = ROWS[t]
                dve.wait_ge(S["o_sq"], t + 1)
                dve.tensor_scalar(ss[0:r, 0:H], ss[0:r, 0:H], 1.0 / P, EPS, ALU.mult, ALU.add).then_inc(S["o_ms"], 1)
                dve.wait_ge(S["o_rms"], t + 1)
                if t >= 2:
                    dve.wait_ge(S["mix_tr"], t - 1)
                link(dve.reciprocal(rs[0:r, 0:H], rs[0:r, 0:H]))
                for h in range(H):
                    hs = slice(h * P, (h + 1) * P)
                    ins = dve.scalar_tensor_tensor(out=mtok[t % 2][0:r, hs], in0=ps[4 + t % 2][0:r, hs], scalar=rs[0:r, h:h + 1],
                                                   in1=Gt[0:r, t, hs], op0=ALU.mult, op1=ALU.mult)
                ins.then_inc(S["o_norm"], 1)

            mask(0)
            for t in range(PT):
                for j in range(4):
                    c = 4 * t + j
                    dve.wait_ge(S["u_mm"], c + 1)
                    new, old, U = Sr[(c + 1) % 3], Sr[c % 3], ps[6 + c % 2].rearrange("p (h v) -> p h v", h=H)
                    if c == 0:
                        ins = dve.tensor_copy(new, U)
                    else:
                        dve.wait_ge(S["s_upd"], c)
                        for h in range(H):
                            ins = dve.scalar_tensor_tensor(out=new[:, h, :], in0=old[:, h, :], scalar=dl[:, h, c:c + 1],
                                                           in1=U[:, h, :], op0=ALU.mult, op1=ALU.add)
                    ins.then_inc(S["s_upd"], 1)
                if t + 1 < PT:
                    mask(t + 1)
                norm_o(t)
            mask(PT)
            for half in range(2):
                if half == 1:
                    dve.wait_ge(S["us_mm"], 4)
                for b in range(4):
                    dve.tensor_scalar(Vm[0:NS, b, :], V[0:NS, PT, :], seqm[:, 4 * half + b:4 * half + b + 1], None, ALU.mult)
                link(dve.memset(QhM, 0.0))
                for b in range(4):
                    c = TS * (4 * half + b)
                    ins = dve.tensor_copy(QhM[:, :, b, c:c + TS], qT[:, :, TP + c:TP + c + TS])
                ins.then_inc(S["vm_ready"], 1)
                dve.wait_ge(S["s0_in"], 32)
                S0h = S0[half]
                for h in range(H):
                    dve.wait_ge(S["us_mm"], 4 * half + h + 1)
                    link(tt(S0h[:, :, h, :], S0h[:, :, h, :],
                            dls[:, h, 4 * half:4 * half + 4].unsqueeze(2).to_broadcast([P, 4, P]), ALU.mult))
                    ins = tt(S0h[:, :, h, :], S0h[:, :, h, :], ps[6 + h % 2].rearrange("p (b v) -> p b v", b=4), ALU.add)
                    if h < H - 1:
                        ins.then_inc(S["s_upd"], 1)
                ins.then_inc(S["s0_new"], 1)
            norm_o(PT)

            for m in range(SF):
                dve.wait_ge(S["glu_sig"], m + 1)
                link(tt(y2[:, m, :], y2[:, m, :], uT[:, m, :], ALU.mult))
                tt(sqy[:, m, :], y2[:, m, :], y2[:, m, :], ALU.mult).then_inc(S["glu_sq"], 1)
            dve.wait_ge(S["glu_ss"], 1)
            dve.tensor_scalar(rsy[:, 0:TP], ps[6][:, :], 1.0 / DH, EPS, ALU.mult, ALU.add)
            dve.tensor_scalar(rsy[:, TP:NT], ps[7][:, 0:NS], 1.0 / DH, EPS, ALU.mult, ALU.add).then_inc(S["glu_rt"], 1)
            dve.wait_ge(S["glu_rt"], 2)
            link(dve.reciprocal(rsy, rsy))
            for m in range(SF):
                ins = dve.scalar_tensor_tensor(out=mixT[:, H + m, :], in0=y2[:, m, :], scalar=prm[:, 12 + m:13 + m], in1=rsy,
                                               op0=ALU.mult, op1=ALU.mult)
            ins.then_inc(S["glu_mix"], 1)

            def ffn_gain():
                dve.wait_ge(S["bc_h2"], 16 * 5)
                dve.scalar_tensor_tensor(out=A2b[:, 0, :], in0=A2b[:, 0, :], scalar=1.0, in1=gffn, op0=ALU.add, op1=ALU.mult)
                link(dve.scalar_tensor_tensor(out=A2b[0:NS, 1, :], in0=A2b[0:NS, 1, :], scalar=1.0, in1=gffn[0:NS, :],
                                              op0=ALU.add, op1=ALU.mult))

            dve.wait_ge(S["bc_g1"], 32)
            dve.wait_ge(S["late_in"], 16 * (2 + NG))
            dve.wait_ge(S["xr_in"], 16 * PT)

            def copy_turned(t):
                r = ROWS[t]
                dve.wait_ge(S["tr2"], 2 * t + 1)
                dve.tensor_copy(h2T[:, 0:4, t * P:t * P + r], ps[4 + 2 * (t % 2)].rearrange("p (c t) -> p c t", c=4)[:, :, 0:r])\
                    .then_inc(S["h2_dve"], 1)

            for t in range(TILES):
                r, kind = ROWS[t], int(t == PT)
                dve.wait_ge(S["wo_mm"], t + 1)
                if t >= 2:
                    dve.wait_ge(S["tr2"], 2 * (t - 1))
                    dve.wait_ge(h2_sem[t % 2], 16 * (t // 2))
                tmp = xn2[t % 2][0:r, :]
                for j in range(2):
                    js = slice(512 * j, 512 * j + 512)
                    ins = tt(tmp[:, js], ps[2 * (t % 2) + j][0:r, :], g1b[0:r, kind, js], ALU.mult)
                ins.then_inc(S["wo_t"], 1)
                dve.wait_ge(S["wo_t"], t + 1)
                if t == PT:
                    dve.wait_ge(S["xr_last_in"], 16)
                tt(x[0:r, t, :], x[0:r, t, :], tmp, ALU.add).then_inc(S["x2"], 1)
                if t == 0:
                    ffn_gain()
                if t >= 1:
                    copy_turned(t - 1)
                dve.wait_ge(S["x2_sq"], t + 1)
                dve.tensor_scalar(ss[0:r, t:t + 1], ss[0:r, t:t + 1], 1.0 / D, EPS, ALU.mult, ALU.add).then_inc(S["x2_ms"], 1)
                dve.wait_ge(S["x2_rt"], t + 1)
                link(dve.reciprocal(rs[0:r, t:t + 1], rs[0:r, t:t + 1]))
                link(dve.scalar_tensor_tensor(out=tmp, in0=x[0:r, t, :], scalar=rs[0:r, t:t + 1], in1=A2b[0:r, kind, :],
                                              op0=ALU.mult, op1=ALU.mult))
                tt(tmp, tmp, B2b[0:r, kind, :], ALU.add).then_inc(S["xn2_ready"], 1)
            copy_turned(PT)

            dve.memset(RT["gl"], -1e30)
            link(dve.memset(RT["el"], 0.0))
            dve.memset(RT["gl"][:, :, 0:NG], 0.0)
            dve.wait_ge(S["lg_mm"], 1)
            dve.wait_ge(S["iota"], 2)
            link(dve.memset(RT["st"], 0.0))
            for t in range(TILES):
                r = ROWS[t]
                lg = ps[0][0:r, (NG + E) * t:(NG + E) * (t + 1)]
                tt(RT["gl"][0:r, t, 0:NG], lg[:, 0:NG], brt[0:r, 0:NG], ALU.add)
                ins = tt(RT["el"][0:r, t, :], lg[:, NG:], brt[0:r, NG:], ALU.add)
            ins.then_inc(S["lg_read"], 1)
            dve.wait_ge(S["lg_read"], 1)
            for t in range(TILES):
                ins = dve.max(out=RT["gm8"][:, t, :], in_=RT["gl"][:, t, :])
            link(ins)
            for t in range(TILES):
                ins = dve.max_index(out=RT["gx"][:, t, :].bitcast(U32), in_max=RT["gm8"][:, t, :], in_values=RT["gl"][:, t, :])
            link(ins)
            dve.tensor_scalar(RT["ngm"], RT["gm8"][:, :, 0], -1.0, None, ALU.mult).then_inc(S["rt_exp"], 1)
            link(dve.tensor_copy(RT["gi"], RT["gx"].bitcast(U32)[:, :, 0]))
            link(tt(RT["oh"], iota[:, 0:NG].unsqueeze(1).to_broadcast([P, TILES, NG]),
                    RT["gi"].unsqueeze(2).to_broadcast([P, TILES, NG]), ALU.is_equal))
            for g in range(NG):
                dst = RT["sel"] if g == 0 else RT["st"]
                link(tt(dst, RT["el"][:, :, NE * g:NE * (g + 1)],
                        RT["oh"][:, :, g:g + 1].to_broadcast([P, TILES, NE]), ALU.mult))
                if g:
                    link(tt(RT["sel"], RT["sel"], RT["st"], ALU.add))
            for t in range(TILES):
                ins = dve.max(out=RT["sm8"][:, t, :], in_=RT["sel"][:, t, :])
            link(ins)
            for t in range(TILES):
                dve.max_index(out=RT["sx"][:, t, :].bitcast(U32), in_max=RT["sm8"][:, t, :], in_values=RT["sel"][:, t, :])
            tt(RT["dv"], RT["sm8"][:, :, 1], RT["sm8"][:, :, 0], ALU.subtract).then_inc(S["rt_exp"], 1)
            dve.wait_ge(S["rt_exp"], 2)
            dve.tensor_copy(RT["i0"], RT["sx"].bitcast(U32)[:, :, 0])
            link(dve.tensor_copy(RT["i1"], RT["sx"].bitcast(U32)[:, :, 1]))
            for nm in ("i0", "i1"):
                ins = dve.scalar_tensor_tensor(out=RT[nm], in0=RT["gi"], scalar=float(NE), in1=RT[nm], op0=ALU.mult, op1=ALU.add)
            link(ins)
            io = iota.unsqueeze(1).to_broadcast([P, TILES, E])
            tt(comb, io, RT["i0"].unsqueeze(2).to_broadcast([P, TILES, E]), ALU.is_equal)
            link(tt(cb2, io, RT["i1"].unsqueeze(2).to_broadcast([P, TILES, E]), ALU.is_equal))
            tt(SM, comb, cb2, ALU.add).then_inc(S["SM_ready"], 1)
            for t in range(2, TILES):
                dve.wait_ge(S["SM_ready"], t - 1)
                tt(SMsum[:, t - 2, :], SM[:, 0, :] if t == 2 else SMsum[:, t - 3, :], SM[:, t - 1, :], ALU.add)\
                    .then_inc(S["SM_ready"], 1)
            dve.wait_ge(S["SM_ready"], PT)
            dve.wait_ge(S["rt_exp2"], 1)
            dve.reciprocal(RT["gw"], RT["gs"])
            link(dve.tensor_scalar(RT["w0"], RT["e1"], 1.0, None, ALU.add))
            link(dve.reciprocal(RT["w0"], RT["w0"]))
            link(tt(RT["w0"], RT["w0"], RT["gw"], ALU.mult))
            tt(RT["w1"], RT["w0"], RT["e1"], ALU.mult)
            dve.wait_ge(S["rank_mm"], 1)
            dve.wait_ge(S["iota"], 3)
            dve.tensor_copy(cntf, ps[1][:, TILES * E:(TILES + 1) * E])
            link(dve.memset(rk, 0.0))
            for t in range(TILES):
                r = ROWS[t]
                ins = dve.scalar_tensor_tensor(out=rk[0:r, t, :], in0=ps[1][0:r, E * t:E * (t + 1)], scalar=float(E),
                                               in1=iota[0:r, :], op0=ALU.mult, op1=ALU.add)
            link(ins)
            link(dve.tensor_reduce(flagf, cntf, AX, ALU.max))
            dve.tensor_scalar(flag.bitcast(I32), flagf, float(P), None, ALU.is_gt).then_inc(S["flag"], 1)
            for k in range(2):
                link(tt(SM, (comb, cb2)[k], rk, ALU.mult))
                link(dve.tensor_reduce(pos[k], SM, AX, ALU.add))
                dve.tensor_copy(pos[k].bitcast(U32), pos[k]).then_inc(S["pos"], 1)
            link(dve.memset(yoff[:, 0:1], 0.0))
            link(dve.tensor_copy(yoff[:, 1:E], cntf[:, 0:E - 1]))
            d = 1
            while d < E:
                link(dve.tensor_copy(yix, yoff))
                link(tt(yoff[:, d:E], yix[:, d:E], yix[:, 0:E - d], ALU.add))
                d *= 2
            for t in range(TILES):
                r = ROWS[t]
                ins = tt(rk[0:r, t, :], ps[1][0:r, E * t:E * (t + 1)], yoff[0:r, :], ALU.add)
            link(ins)
            for k in range(2):
                link(tt(SM, (comb, cb2)[k], rk, ALU.mult))
                link(dve.tensor_reduce(ypos[k], SM, AX, ALU.add))
                dve.tensor_copy(ypos[k].bitcast(U32), ypos[k]).then_inc(S["pos"], 1)
            link(tt(yix, cntf, pcol.to_broadcast([P, E]), ALU.is_le))
            link(dve.scalar_tensor_tensor(out=yix, in0=yix, scalar=float(NOWHERE), in1=yoff, op0=ALU.mult, op1=ALU.add))
            link(tt(yix, yix, pcol.to_broadcast([P, E]), ALU.add))
            dve.tensor_copy(yix.bitcast(U32), yix).then_inc(S["pos"], 1)
            tt(comb, comb, RT["w0"].unsqueeze(2).to_broadcast([P, TILES, E]), ALU.mult)
            link(tt(cb2, cb2, RT["w1"].unsqueeze(2).to_broadcast([P, TILES, E]), ALU.mult))
            link(tt(comb, comb, cb2, ALU.add))

            def final_gains():
                dve.wait_ge(S["bc_fin"], 64)
                dve.wait_ge(S["bc_g2"], 32)
                dve.scalar_tensor_tensor(out=cfb[:, 0, :], in0=cfb[:, 0, :], scalar=1.0, in1=gfin, op0=ALU.add, op1=ALU.mult)
                dve.scalar_tensor_tensor(out=cfb[0:NS, 1, :], in0=cfb[0:NS, 1, :], scalar=1.0, in1=gfin[0:NS, :],
                                         op0=ALU.add, op1=ALU.mult).then_inc(S["mod3"], 1)
                dve.wait_ge(S["mod3"], 1)

            dve.wait_ge(S["fin_stored"], 64)
            dve.wait_ge(S["ada_stored"], 128)
            def gate2(t):
                r, kind = ROWS[t], int(t == PT)
                tt(acc[0:r, t, :], acc[0:r, t, :], g2b[0:r, kind, :], ALU.mult).then_inc(S["gated"], 1)
                dve.wait_ge(S["gated"], t + 1)
                tt(x[0:r, t, :], x[0:r, t, :], acc[0:r, t, :], ALU.add).then_inc(S["x3"], 1)

            dense = dve.value_load(flag[0:1, :].bitcast(I32), min_val=0, max_val=1)
            with dve.If(dense > 0):
                dve.wait_ge(h2_sem[0], 16 * 3)
                dve.wait_ge(h2_sem[1], 16 * 2)
                dve.memset(at(MAIN + TILES * D, TILES * D), 0.0).then_inc(S["acc_zero"], 1)
                dve.wait_ge(S["acc_zero"], 1)
                with dve.Fori(0, E // 4) as i:
                    base = i * (4 * TILES)

                    def act_unit(k):
                        r = ROWS[k % TILES]
                        dve.wait_ge(S["g_sig"], base + (k + 1))
                        tt(aa[k % 2][0:r, :], ps[k % 2][0:r, 0:DE], sg[k % 2][0:r, :], ALU.mult).then_inc(S["gs_mul"], 1)
                        dve.wait_ge(S["gs_mul"], base + (k + 1))
                        tt(aa[k % 2][0:r, :], ps[k % 2][0:r, DE:], aa[k % 2][0:r, :], ALU.mult).then_inc(S["act_ready"], 1)

                    act_unit(0)
                    for k in range(4 * TILES):
                        t, r = k % TILES, ROWS[k % TILES]
                        if k + 1 < 4 * TILES:
                            act_unit(k + 1)
                        dve.wait_ge(S["y_mm"], base + (k + 1))
                        w = comb[0:r, t, :][:, bass.ds(i * 4 + k // TILES, 1)]
                        for j in range(2):
                            js = slice(512 * j, 512 * j + 512)
                            ins = dve.scalar_tensor_tensor(out=acc[0:r, t, js], in0=ps[4 + 2 * (k % 2) + j][0:r, :], scalar=w,
                                                           in1=acc[0:r, t, js], op0=ALU.mult, op1=ALU.add)
                        ins.then_inc(S["y_acc"], 1)

                dve.wait_ge(S["y_acc"], E * TILES)
                final_gains()
                for t in range(TILES):
                    gate2(t)
            with dve.Else():
                def turned(base, k):
                    dve.wait_ge(S["xt_mm"], 2 * base + 2 * k + 1)
                    dve.tensor_copy(xT[k % 2][:, 0:4, :].rearrange("p c t -> p (c t)"), ps[0][:, :]).then_inc(S["xt_dve"], 1)

                def acts(base, k):
                    dve.wait_ge(S["g_sig"], base + (k + 1))
                    tt(aa[k % 2], ps[2 + k % 2][:, 0:DE], sg[k % 2], ALU.mult).then_inc(S["gs_mul"], 1)
                    dve.wait_ge(S["gs_mul"], base + (k + 1))
                    tt(aa[k % 2], ps[2 + k % 2][:, DE:], aa[k % 2], ALU.mult).then_inc(S["act_ready"], 1)

                def four(base, first, last):
                    for k in range(4):
                        if not (last and k == 3):
                            acts(base, k + 1)
                        if not (last and k >= 2):
                            turned(base, k + 2)
                        dve.wait_ge(S["y_mm"], base + (k + 1))
                        if not (first and k < 2):
                            dve.wait_ge(S[f"ys{k % 2}"], base * 8 + 16 * (k // 2))
                        dve.tensor_copy(yb[k % 2][:, 512:], ps[7][:, :]).then_inc(S["yb_dve"], 1)

                turned(0, 0)
                acts(0, 0)
                turned(0, 1)
                four(0, True, False)
                with dve.Fori(1, E // 4 - 1) as i:
                    four(i * 4, False, False)
                four(E - 4, False, True)
                final_gains()
                for t in range(TILES):
                    r = ROWS[t]
                    dve.wait_ge(fin_in[t], 32)
                    dve.wait_ge(S["y0_scaled"], t + 1)
                    dve.scalar_tensor_tensor(out=acc[0:r, t, :], in0=y1[t][0:r, :], scalar=RT["w1"][0:r, t:t + 1],
                                             in1=acc[0:r, t, :], op0=ALU.mult, op1=ALU.add).then_inc(S["comb2"], 1)
                    dve.wait_ge(S["comb2"], t + 1)
                    gate2(t)

            dve.wait_ge(S["x3_sq"], TILES)
            dve.tensor_scalar(ss[:, 0:TILES], ss[:, 0:TILES], 1.0 / D, EPS, ALU.mult, ALU.add).then_inc(S["x3_ms"], 1)
            dve.wait_ge(S["x3_rt"], 1)
            link(dve.reciprocal(rs[:, 0:TILES], rs[:, 0:TILES]))
            for t in range(TILES):
                r, kind = ROWS[t], int(t == PT)
                link(dve.scalar_tensor_tensor(out=x[0:r, t, :], in0=x[0:r, t, :], scalar=rs[0:r, t:t + 1],
                                              in1=cfb[0:r, kind, :], op0=ALU.mult, op1=ALU.mult))
                tt(x[0:r, t, :], x[0:r, t, :], sfb[0:r, kind, :], ALU.add).then_inc(S["y_ready"], 1)

        @block.tensor
        def _(pe):
            def mm(out, lhsT, rhs, start, stop):
                return pe.matmul(out, lhsT, rhs, start=start, stop=stop, skip_group_check=True)

            ada_n = [0]

            def ada_bank():
                ada_n[0] += 1
                if ada_n[0] > 2:
                    pe.wait_ge(S["ada_out"], ada_n[0] - 2)
                return ps[(ada_n[0] - 1) % 2]

            piece = [0]

            def next_piece():
                p_ = piece[0]
                piece[0] += 1
                pe.wait_ge(landed[p_ % 4], 16 * (p_ // 4 + 1))
                return slot[p_ % 4].rearrange("p (c n) -> p c n", c=KC)

            pe.wait_ge(S["identity"], 1)
            pe.wait_ge(S["cact"], 1)
            bank = ada_bank()
            for c in range(KC):
                ins = pe.transpose(bank[:, C9 * c:C9 * (c + 1)], c9[:, c:D:KC], ident[0:C9, 0:C9])
            ins.then_inc(S["ada_mm"], 1)
            bank = ada_bank()
            pe.wait_ge(S["prm_in"], 16 * 10)
            pe.transpose(bank[:, 0:PARAMS], prow, ident[0:PARAMS, 0:PARAMS]).then_inc(S["ada_mm"], 1)
            pe.wait_ge(S["ada_out"], 1)

            def ada_row(v, h):
                bank = ada_bank()
                w = next_piece()
                q = 32 * (v % 4)
                for c in range(KC):
                    ins = mm(bank[q:q + C9, :], cT[:, c, :], w[:, c, :], c == 0, False)
                j = 2 * v + h
                mm(bank[q:q + C9, :], ident[0:16, j:j + 1].to_broadcast([16, C9]), bias16, False, True).then_inc(S["ada_mm"], 1)

            def ada_col(v):
                bank = ada_bank()
                pe.wait_ge(S["ada_out"], ada_n[0] - 1)
                q = 32 * (v % 4)
                for c in range(KC):
                    ins = pe.transpose(bank[:, C9 * c:C9 * (c + 1)], rows8[q:q + C9, v // 4, c:D:KC], ident[q:q + C9, q:q + C9])
                ins.then_inc(S["ada_mm"], 1)



            def turn_tile(t, src, banks, done):
                r = ROWS[t]
                for c in range(KC):
                    ins = pe.transpose(banks[c // 4][:, P * (c % 4):P * (c % 4) + r], src[0:r, c:D:KC], ident[0:r, 0:r])
                    if c % 4 == 3:
                        ins.then_inc(done, 1)

            def turn_x(t):
                pe.wait_ge(S["xn_ready"], t + 1)
                if t >= 2:
                    pe.wait_ge(S["h_dve"], t - 1)
                    pe.wait_ge(S["h_act"], t - 1)
                turn_tile(t, xin[:, t, :], (ps[2 + 2 * (t % 2)], ps[3 + 2 * (t % 2)]), S["tr_h"])

            for v, h in ADA[:3]:
                ada_row(v, h)
            turn_x(0)
            turn_x(1)
            ada_row(*ADA[3])
            ada_col(0)
            ada_col(1)
            for t in range(2, TILES):
                turn_x(t)

            pe.wait_ge(S["h_dve"], TILES)
            pe.wait_ge(S["h_act"], PT)
            w_now = [None]

            def proj_cols(unit):
                if unit % 4 == 0:
                    w_now[0] = next_piece()
                w, m = w_now[0], unit % 4
                if unit < 4:
                    if unit == 3:
                        pe.wait_ge(S["proj_act"], 1)
                    b0, b1 = ps[2 + 2 * (unit % 3)], ps[3 + 2 * (unit % 3)]
                else:
                    pe.wait_ge(S["ada_out"], 8)
                    pe.wait_ge(S["proj_act"], unit)
                    b0, b1 = ps[0], ps[1]
                for c in range(KC):
                    lhs = w[:, c, m * P:(m + 1) * P]
                    mm(b0[:, :], lhs, hT[:, c, 0:TP], c == 0, c == KC - 1)
                    ins = mm(b1[:, 0:NS], lhs, hT[:, c, TP:NT], c == 0, c == KC - 1)
                ins.then_inc(S["proj_mm"], 1)

            def proj_rows(unit):
                if unit in (12, 17):
                    w_now[0] = next_piece()
                w, t = w_now[0], (unit - 12) % TILES
                r = ROWS[t]
                if unit >= 16:
                    pe.wait_ge(S["proj_act"], unit - 3)
                if unit == 21:
                    pe.wait_ge(S["proj_dve"], 1)
                for c in range(KC):
                    ins = mm(ps[4 + unit % 4][0:r, :], hT[:, c, t * P:t * P + r], w[:, c, :], c == 0, c == KC - 1)
                ins.then_inc(S["proj_mm"], 1)

            for unit in range(4):
                proj_cols(unit)

            pe.wait_ge(S["bc_in"], 16 * 12)
            pe.wait_ge(S["proj_act"], 3)
            for k in range(2):
                for half in range(2):
                    ins = pe.transpose(ps[6][:, 256 * k + P * half:256 * k + P * (half + 1)], crow[:, 2 * k + half, :], ident)
                ins.then_inc(S["bc_tr"], 1)
            for k in range(2):
                pe.transpose(ps[7][:, P * k:P * (k + 1)], xrow[:, k, :], ident).then_inc(S["bc_tr"], 1)

            beside = [(4, 5), (6, 7), (8, 9), (10, 11), ADA_S5[0:2], ADA_S5[2:3], ADA_S5[3:5], ADA_S5[5:6]]

            def beside_s5(j):
                if j == 4:
                    pe.wait_ge(S["proj_act"], 12)
                for w in beside[j]:
                    ada_row(*w) if j >= 4 else proj_cols(w)

            pe.wait_ge(S["const"], 1)
            pe.wait_ge(S["proj_act"], 4)
            for r in range(SF):
                beside_s5(2 * r)
                pe.wait_ge(S["s5_mat"], r + 1)
                if r >= 1:
                    pe.wait_ge(S["s5_X"], r)
                if r >= 1:
                    pe.wait_ge(S["s5_Yout"], 16 * r)
                for k in range(2):
                    for hf in range(2):
                        for q in range(2):
                            for a_ in range(2):
                                c0 = P * (2 * q + a_)
                                ins = pe.transpose(ps[2 + 2 * k + hf][:, c0:c0 + P],
                                                   AB[k][:, 2 * hf + q, 4 * a_:4 * a_ + 4, :].rearrange("p s h -> p (s h)"), ident)
                        ins.then_inc(S["s5_tr"], 1)
                pe.wait_ge(S["bc_out"], 4)
                pe.wait_ge(S["s5_ca"], r + 1)
                for hf in range(2):
                    for q in range(2):
                        qq = 2 * hf + q
                        for k in range(2):
                            ins = mm(ps[6 + hf][0:32, 256 * q:256 * q + 256], AB[k][:, qq, L - 1, :],
                                     CA[k][:, qq, 0:L, :].rearrange("p j h -> p (j h)"), k == 0, k == 1)
                    ins.then_inc(S["s5_T"], 1)
                pe.wait_ge(S["s5_trout"], 4 * (r + 1))
                pe.wait_ge(S["s5_U"], r + 1)
                pe.wait_ge(S["s5_Up"], r + 1)
                for k in range(2):
                    for q in range(4):
                        for a_ in range(2):
                            ins = mm(ps[2 + k][:, NC * q:NC * (q + 1)], Bl[k][:, q, a_, :], Um[:, q, a_, :], a_ == 0, a_ == 1)
                ins.then_inc(S["s5_W"], 1)
                beside_s5(2 * r + 1)
                pe.wait_ge(S["s5_D"], r + 1)
                pe.wait_ge(S["s5_X"], r + 1)
                for q in range(4):
                    for b in range(2):
                        out = ps[4 + q // 2][:, 144 * (q % 2) + NC * b:144 * (q % 2) + NC * (b + 1)]
                        for a_ in range(b + 1):
                            mm(out, Tm[:, q, P * (b - a_):P * (b - a_ + 1)], Um[:, q, a_, :], a_ == 0, False)
                        for k in range(2):
                            ins = mm(out, CA[k][:, q, 4 * b + 1:4 * b + 5, :].rearrange("p j h -> p (j h)"), Xb[k][:, q, :],
                                     False, k == 1)
                    if q % 2:
                        ins.then_inc(S["s5_Y"], 1)
            for k in range(2):
                pe.transpose(ps[2 + k][:, 0:P], fin[k][:, 0:NB, :].rearrange("p b r -> p (b r)"), ident)
                pe.transpose(ps[2 + k][0:NPAIR, P:2 * P], fin[k][:, NB, :], ident).then_inc(S["s5_fintr"], 1)

            pe.wait_ge(S["s5_finout"], 2)
            pe.wait_ge(S["s5_Yout"], 16 * SF)
            for h in range(H):
                for unit in (12, 13, 14) if h < 3 else (12,):
                    proj_rows(unit + 3 * h)
                if h == 3:
                    for w in ADA_HGRN:
                        ada_row(*w)
                pe.wait_ge(S["hprep"], h + 1)
                if h >= 1:
                    pe.wait_ge(S["kh_out"], h)
                for t in range(PT):
                    pe.transpose(ps[2][:, P * t:P * (t + 1)], Kh[:, P * t:P * (t + 1)], ident)
                pe.transpose(ps[3][0:NS, 0:P], Kh[:, TP:NT], ident).then_inc(S["kh_tr"], 1)
            pe.wait_ge(S["kh_out"], H)

            def scores(t):
                r = ROWS[t]
                if t >= 1:
                    pe.wait_ge(S["sc_mask"], t)
                for h in range(H):
                    ts = slice(t * P, t * P + r)
                    ins = mm(ps[2][0:r, P * h:P * h + r], fT[:, h, ts], Qt[:, h, ts], True, True)
                ins.then_inc(S["sc_mm"], 1)

            scores(0)
            pe.wait_ge(S["proj_act"], 22)
            pe.wait_ge(S["proj_dve"], TILES)
            for t in range(TILES):
                r = ROWS[t]
                ob = ps[4 + t % 2]
                pe.wait_ge(S["sc_mask"], t + 1)
                if t >= 2:
                    pe.wait_ge(S["o_norm"], t - 1)
                for h in range(H):
                    mm(ob[0:r, P * h:P * (h + 1)], sT[t % 2][0:r, h, 0:r], V[0:r, t, P * h:P * (h + 1)], h == 0, False)
                if t < PT:
                    for j in range(4):
                        c = 4 * t + j
                        js = slice(32 * j, 32 * j + 32)
                        if c >= 2:
                            pe.wait_ge(S["s_upd"], c - 1)
                        for h in range(H):
                            hs = slice(P * h, P * (h + 1))
                            ins = mm(ps[6 + c % 2][:, hs], KhT[js, t, hs], V[js, t, hs], True, True)
                        ins.then_inc(S["u_mm"], 1)
                        if c >= 1:
                            pe.wait_ge(S["s_upd"], c)
                            for h in range(H):
                                ins = mm(ob[js, P * h:P * (h + 1)], qT[:, h, t * P + 32 * j:t * P + 32 * j + 32], Sr[c % 3][:, h, :],
                                         False, True)
                    ins.then_inc(S["o_mm"], 1)
                    scores(t + 1)
                else:
                    for half in range(2):
                        pe.wait_ge(S["vm_ready"], half + 1)
                        pe.wait_ge(S["s0_in"], 32)
                        for b in range(4):
                            for h in range(H):
                                ins = mm(ob[0:NS, P * h:P * (h + 1)], QhM[:, h, b, :], S0[half][:, b, h, :], False, True)
                        if half == 1:
                            ins.then_inc(S["o_mm"], 1)
                        for h in range(H):
                            done = NCH + 3 * half
                            if h == 0:
                                pe.wait_ge(S["s_upd"], done)
                            if half == 1 and h < 2:
                                pe.wait_ge(S["s0_new"], 1)
                            if h >= 2:
                                pe.wait_ge(S["s_upd"], done + h - 1)
                            mm(ps[6 + h % 2][:, :], KhT[0:NS, PT, P * h:P * (h + 1)], Vm[0:NS, :, P * h:P * (h + 1)], True, True)\
                                .then_inc(S["us_mm"], 1)
                pe.wait_ge(S["o_norm"], t + 1)
                if t >= 1:
                    pe.wait_ge(S["mix_out"], t)
                for h in range(H):
                    ins = pe.transpose(ps[3][:, P * h:P * h + r], mtok[t % 2][0:r, P * h:P * (h + 1)], ident[0:r, 0:r])
                ins.then_inc(S["mix_tr"], 1)

            pe.wait_ge(S["mix_out"], TILES)
            w = next_piece()
            w = slot[GLU_PIECE % 4][:, 0:4 * DH].rearrange("p (c n) -> p c n", c=4)
            for m in range(SF):
                if m >= 2:
                    pe.wait_ge(S["glu_sig"], m - 1)
                for c in range(SF):
                    lhs = w[:, c, m * P:(m + 1) * P]
                    mm(ps[2 + 2 * (m % 2)][:, :], lhs, uT[:, c, 0:TP], c == 0, c == SF - 1)
                    ins = mm(ps[3 + 2 * (m % 2)][:, 0:NS], lhs, uT[:, c, TP:NT], c == 0, c == SF - 1)
                ins.then_inc(S["glu_mm"], 1)
            pe.wait_ge(S["ada_out"], 16)
            w_out = (next_piece(), next_piece())

            def out_part(t, j, cs):
                r = ROWS[t]
                for c in cs:
                    ins = mm(ps[2 * (t % 2) + j][0:r, :], mixT[:, c, t * P:t * P + r], w_out[j][:, c, :], c == 0, c == KC - 1)
                return ins

            out_part(0, 0, range(H))
            pe.wait_ge(S["s0_new"], 2)
            for m in range(SF):
                pe.wait_ge(S["glu_sq"], m + 1)
                mm(ps[6][:, :], ones, sqy[:, m, 0:TP], m == 0, m == SF - 1)
                ins = mm(ps[7][:, 0:NS], ones, sqy[:, m, TP:NT], m == 0, m == SF - 1)
            ins.then_inc(S["glu_ss"], 1)
            out_part(0, 1, range(H))
            pe.wait_ge(S["glu_sig"], SF - 1)
            out_part(1, 0, range(H))
            out_part(1, 1, range(H))

            pe.wait_ge(S["glu_mix"], 1)

            def out_proj(t):
                if t >= 2:
                    pe.wait_ge(S["wo_t"], t - 1)
                for j in range(2):
                    ins = out_part(t, j, range(H if t < 2 else 0, KC))
                ins.then_inc(S["wo_mm"], 1)

            def late_row(j):
                v, h = ADA_ROUTER[j]
                w = next_piece()
                if j >= 2:
                    pe.wait_ge(S["ada_out"], 16 + j - 1)
                q = 32 * (v % 4)
                for c in range(KC):
                    mm(ps[2 + h][q:q + C9, :], cT[:, c, :], w[:, c, :], c == 0, False)
                jj = 2 * v + h
                mm(ps[2 + h][q:q + C9, :], ident[0:16, jj:jj + 1].to_broadcast([16, C9]), bias16, False, True)\
                    .then_inc(S["ada_mm"], 1)

            def router_logits(out, t0, t1):
                for c in range(KC):
                    ins = mm(out, wrc[:, c, :], h2T[:, c, t0:t1], c == 0, c == KC - 1)
                ins.then_inc(S["lgT_mm"], 1)

            out_proj(0)
            for t in range(TILES):
                if t + 1 < TILES:
                    out_proj(t + 1)
                if t == PT:
                    pe.wait_ge(S["wo_t"], PT)
                    late_row(0)
                    late_row(1)
                    pe.wait_ge(S["iota"], 2)
                    pe.wait_ge(S["wo_t"], TILES)
                    pe.wait_ge(S["h2_dve"], PT)
                    pe.wait_ge(S["h2_act"], PT)
                    router_logits(ps[0][0:LG, :], 0, TP)
                pe.wait_ge(S["xn2_ready"], t + 1)
                if t >= 2:
                    pe.wait_ge(S["h2_dve"], t - 1)
                    pe.wait_ge(S["h2_act"], t - 1)
                turn_tile(t, xn2[t % 2], (ps[4 + 2 * (t % 2)], ps[5 + 2 * (t % 2)]), S["tr2"])

            pe.wait_ge(S["h2_dve"], TILES)
            pe.wait_ge(S["h2_act"], TILES)
            router_logits(ps[1][0:LG, 0:NS], TP, NT)
            pe.wait_ge(S["lgT_out"], 2)
            for t in range(TILES):
                r = ROWS[t]
                ins = pe.transpose(ps[0][0:r, LG * t:LG * (t + 1)], lgT[:, t * P:t * P + r], ident[0:LG, 0:LG])
            ins.then_inc(S["lg_mm"], 1)
            def ranks():
                pe.wait_ge(S["before"], 1)
                for t in range(TILES + 1):
                    r = ROWS[t] if t < TILES else P
                    out = ps[1][0:r, E * t:E * (t + 1)]
                    pe.wait_ge(S["SM_ready"], max(1, min(t, PT)))
                    if t < TILES:
                        mm(out, before[0:r, 0:r], SM[0:r, t, :], True, t == 0)
                    else:
                        mm(out, ones[0:NS, :], SM[0:NS, PT, :], True, False)
                    if t:
                        ins = mm(out, ones[:, 0:r], SM[:, 0, :] if t == 1 else SMsum[:, min(t, PT) - 2, :], False, True)
                ins.then_inc(S["rank_mm"], 1)

            late_row(2)
            late_row(3)
            ranks()

            pe.wait_ge(S["ada_out"], 20)
            pe.wait_ge(S["lg_read"], 1)
            pe.wait_ge(S["flag"], 1)
            pe.wait_ge(S["pos"], 4)

            dense = pe.value_load(flag[0:1, :].bitcast(I32), min_val=0, max_val=1)
            with pe.If(dense > 0):
                with pe.Fori(0, E // 4) as i:
                    base = i * (4 * TILES)

                    def gate_up(k):
                        e4, t = divmod(k, TILES)
                        r = ROWS[t]
                        s = (0, 1, 3, 4)[e4]
                        if t == 0:
                            pe.wait_ge(landed[s], i * 32 + ((16 * (N0 // 4) if s < 4 else 0) + 32))
                        if k >= 2:
                            pe.wait_ge(S["act_ready"], base + (k - 1))
                        w = slot[s].rearrange("p (b c f) -> p c b f", b=2, c=KC)
                        for c in range(KC):
                            ins = mm(ps[k % 2][0:r, :].rearrange("p (b f) -> p b f", b=2), h2T[:, c, t * P:t * P + r], w[:, c],
                                     c == 0, c == KC - 1)
                        ins.then_inc(S["gu_mm"], 1)

                    gate_up(0)
                    for k in range(4 * TILES):
                        e4, t = divmod(k, TILES)
                        r = ROWS[t]
                        if k + 1 < 4 * TILES:
                            gate_up(k + 1)
                        pe.wait_ge(S["act_ready"], base + (k + 1))
                        for f in range(2):
                            ins = pe.transpose(ps[2 + k % 2][:, P * f:P * f + P], aa[k % 2][:, f:DE:2], ident)
                        ins.then_inc(S["at_mm"], 1)
                        s = (2, 5)[e4 // 2]
                        if t == 0 and e4 % 2 == 0:
                            pe.wait_ge(landed[s], i * 32 + ((16 * (N0 // 4) if s < 4 else 0) + 32))
                        pe.wait_ge(S["at_out"], base + (k + 1))
                        if k >= 2:
                            pe.wait_ge(S["y_acc"], base + (k - 1))
                        w = slot[s].rearrange("p (e c n) -> p e c n", e=2, c=2)[:, e4 % 2]
                        for j in range(2):
                            for f in range(2):
                                ins = mm(ps[4 + 2 * (k % 2) + j][0:r, :], aT[k % 2][:, f, 0:r], w[:, f, 512 * j:512 * j + 512],
                                         f == 0, f == 1)
                        ins.then_inc(S["y_mm"], 1)
            with pe.Else():
                def landed_at(s):
                    return (16 * (N0 // 4) if s < 4 else 0) + 32

                def turn(base, k):
                    pe.wait_ge(S[f"xg{k % 2}"], base * 8 + 16 * (k // 2 + 1))
                    if not (isinstance(base, int) and base + k == 0):
                        pe.wait_ge(S["xt_dve"], base + k)
                        pe.wait_ge(S["xt_act"], base + k)
                    turn_tile(0, xg[k % 2], (ps[0], ps[1]), S["xt_mm"])

                def gate_up(base, k):
                    s = (0, 1, 3, 4)[k % 4]
                    pe.wait_ge(landed[s], base * 8 + (32 * (k // 4) + landed_at(s)))
                    pe.wait_ge(S["xt_dve"], base + (k + 1))
                    pe.wait_ge(S["xt_act"], base + (k + 1))
                    if not (isinstance(base, int) and base + k < 2):
                        pe.wait_ge(S["act_ready"], base + (k - 1))
                    w = slot[s].rearrange("p (b c f) -> p c b f", b=2, c=KC)
                    for c in range(KC):
                        ins = mm(ps[2 + k % 2][:, :].rearrange("p (b f) -> p b f", b=2), xT[k % 2][:, c, :], w[:, c],
                                 c == 0, c == KC - 1)
                    ins.then_inc(S["gu_mm"], 1)

                def turn_act(base, k):
                    pe.wait_ge(S["act_ready"], base + (k + 1))
                    if not (isinstance(base, int) and base + k < 2):
                        pe.wait_ge(S["at_out"], base + (k - 1))
                    for f in range(2):
                        ins = pe.transpose(ps[4 + k % 2][:, P * f:P * (f + 1)], aa[k % 2][:, f:DE:2], ident)
                    ins.then_inc(S["at_mm"], 1)

                def down(base, k):
                    s = (2, 5)[k // 2]
                    pe.wait_ge(landed[s], base * 8 + landed_at(s))
                    pe.wait_ge(S["at_out"], base + (k + 1))
                    if not (isinstance(base, int) and base + k == 0):
                        pe.wait_ge(S["yb_act"], base + k)
                        pe.wait_ge(S["yb_dve"], base + k)
                    w = slot[s].rearrange("p (e c n) -> p e c n", e=2, c=2)[:, k % 2]
                    for j in range(2):
                        for f in range(2):
                            ins = mm(ps[6 + j][:, :], aT[k % 2][:, f, :], w[:, f, 512 * j:512 * j + 512], f == 0, f == 1)
                    ins.then_inc(S["y_mm"], 1)

                def four(base, last):
                    for k in range(4):
                        turn_act(base, k)
                        if not (last and k == 3):
                            gate_up(base, k + 1)
                        if not (last and k >= 2):
                            turn(base, k + 2)
                        down(base, k)

                turn(0, 0)
                gate_up(0, 0)
                turn(0, 1)
                four(0, False)
                with pe.Fori(1, E // 4 - 1) as i:
                    four(i * 4, False)
                four(E - 4, True)


_OUTS = [("y_prompt", (1, 512, 1024)), ("y_sample", (8, 8, 1024)), ("hgrn_prompt", (1, 1, 4, 128, 128)),
         ("ssm_re_prompt", (1, 1, 32, 64)), ("ssm_im_prompt", (1, 1, 32, 64)), ("hgrn_sample", (1, 8, 4, 128, 128)),
         ("ssm_re_sample", (1, 8, 32, 64)), ("ssm_im_sample", (1, 8, 32, 64))]


def kernel(**inputs):
    import numpy as _np
    import concourse.bacc as _bacc
    from concourse import mybir as _mybir
    from concourse.bass_utils import run_bass_kernel_spmd as _run

    nc = _bacc.Bacc("TRN2", target_bir_lowering=False, num_devices=1)
    arrays, a, o = {}, {}, {}
    for name, value in inputs.items():
        value = _np.ascontiguousarray(value)
        arrays[f"in_{name}"] = value
        a[name] = nc.dram_tensor(f"in_{name}", value.shape, _mybir.dt.from_np(value.dtype), kind="ExternalInput").ap()
    for name, shape in _OUTS:
        o[name] = nc.dram_tensor(f"out_{name}", shape, _mybir.dt.float32, kind="ExternalOutput").ap()
    decoder_step(nc, a, o)
    r = _run(nc, [arrays], core_ids=[0])
    return tuple(r.results[0][f"out_{name}"] for name, _ in _OUTS)
```
